# Optimizing a Trainium2 kernel written in Bass

```python
import jax
import jax.numpy as jnp
from jax import lax
import numpy as np

D_MODEL = 2048
BATCH = 1
SEQ = 256
DEPTH = 2

HEAD_DIM = 128
N_HEADS = D_MODEL // HEAD_DIM
A_HEADS = N_HEADS // 4
B_HEADS = N_HEADS // 4
C_HEADS = N_HEADS - A_HEADS - B_HEADS
IDX_HEADS = 16
IDX_DIM = 64
DSA_TOPK_MAX = 256
DILATED_PATTERNS = ((128, 1), (512, 4), (2048, 16))
C_KV_GROUPS = 2
C_GROUP_SIZE = C_HEADS // C_KV_GROUPS
CMP_BLOCK = 32
CMP_STRIDE = 16
CMP_HIDDEN = 256
SEL_BLOCK = 64
SEL_COUNT = 16
WIN_SIZE = 512
BAND_BLOCK = 128
Q_BLOCK = 128
SEL_Q_CHUNK = 32
D_FF = ((8 * D_MODEL + 2) // 3 + 255) // 256 * 256
ROPE_THETA = 10000.0
RMS_EPS = 1e-6
ATTN_SCALE = HEAD_DIM ** -0.5

IN_WIDTHS = (
    A_HEADS * HEAD_DIM, HEAD_DIM, HEAD_DIM,
    IDX_HEADS * IDX_DIM, IDX_DIM, IDX_HEADS,
    B_HEADS * HEAD_DIM, B_HEADS * HEAD_DIM, B_HEADS * HEAD_DIM,
    C_HEADS * HEAD_DIM,
    C_KV_GROUPS * HEAD_DIM, C_KV_GROUPS * HEAD_DIM,
    C_KV_GROUPS * HEAD_DIM, C_KV_GROUPS * HEAD_DIM,
    C_KV_GROUPS * HEAD_DIM, C_KV_GROUPS * HEAD_DIM,
    3 * C_HEADS,
)
IN_WIDTH = sum(IN_WIDTHS)

kernel_name = "hybrid_dsa_dilated_nsa_block"

def rms_norm(x, g):
    xf = x.astype(jnp.float32)
    y = xf * lax.rsqrt(jnp.mean(xf * xf, axis=-1, keepdims=True) + RMS_EPS)
    return (y * g.astype(jnp.float32)).astype(x.dtype)

def rope_tables(seq_len, dim):
    inv = 1.0 / (ROPE_THETA ** (jnp.arange(0, dim, 2, dtype=jnp.float32) / dim))
    ang = jnp.arange(seq_len, dtype=jnp.float32)[:, None] * inv[None, :]
    return jnp.cos(ang), jnp.sin(ang)

def apply_rope(x, cos, sin):
    xf = x.astype(jnp.float32)
    x1, x2 = jnp.split(xf, 2, axis=-1)
    return jnp.concatenate([x1 * cos - x2 * sin, x2 * cos + x1 * sin], axis=-1).astype(x.dtype)

def banded_attention(q, k, v, max_dist, blk):
    n, r, length, dh = q.shape
    nb = length // blk
    n_prev = -(-max_dist // blk)
    pad = ((0, 0), (n_prev * blk, 0), (0, 0))
    kb = jnp.pad(k, pad).reshape(n, nb + n_prev, blk, dh)
    vb = jnp.pad(v, pad).reshape(n, nb + n_prev, blk, dh)
    kw = jnp.concatenate([kb[:, i:i + nb] for i in range(n_prev + 1)], axis=2)
    vw = jnp.concatenate([vb[:, i:i + nb] for i in range(n_prev + 1)], axis=2)
    width = (n_prev + 1) * blk
    qb = q.reshape(n, r, nb, blk, dh)
    s = jnp.einsum('nrbqd,nbkd->nrbqk', qb, kw).astype(jnp.float32) * dh ** -0.5
    dist = n_prev * blk + jnp.arange(blk)[:, None] - jnp.arange(width)[None, :]
    kglob = (jnp.arange(nb)[:, None] - n_prev) * blk + jnp.arange(width)[None, :]
    mask = ((dist >= 0) & (dist <= max_dist))[None] & (kglob >= 0)[:, None, :]
    s = jnp.where(mask, s, -jnp.inf)
    mx = jnp.max(s, axis=-1, keepdims=True)
    e = jnp.exp(s - mx)
    den = jnp.sum(e, axis=-1, keepdims=True)
    o = jnp.einsum('nrbqk,nbkd->nrbqd', e, vw.astype(jnp.float32)) / den
    lse = (mx + jnp.log(den))[..., 0]
    return o.reshape(n, r, length, dh), lse.reshape(n, r, length)

def dilated_attention(q, k, v, window, dilation):
    b, h, s, dh = q.shape
    unit = dilation * BAND_BLOCK
    s_pad = -(-s // unit) * unit
    m = s_pad // dilation

    def split(t):
        t = jnp.pad(t, ((0, 0), (0, 0), (0, s_pad - s), (0, 0)))
        return t.reshape(b, h, m, dilation, dh).transpose(0, 1, 3, 2, 4).reshape(b * h * dilation, m, dh)

    o, lse = banded_attention(split(q)[:, None], split(k), split(v), window // dilation, BAND_BLOCK)
    o = o.reshape(b, h, dilation, m, dh).transpose(0, 1, 3, 2, 4).reshape(b, h, s_pad, dh)[:, :, :s]
    lse = lse.reshape(b, h, dilation, m).transpose(0, 1, 3, 2).reshape(b, h, s_pad)[:, :, :s]
    return o, lse

def dilated_mixture(q, k, v):
    outs, lses = [], []
    for window, dilation in DILATED_PATTERNS:
        o, lse = dilated_attention(q, k, v, window, dilation)
        outs.append(o)
        lses.append(lse)
    wts = jax.nn.softmax(jnp.stack(lses, axis=0), axis=0)
    return jnp.sum(wts[..., None] * jnp.stack(outs, axis=0), axis=0)

def dsa_attention(q, k, v, iq, ik, iw):
    b, ha, s, dh = q.shape
    topk = min(DSA_TOPK_MAX, s // 4)
    n_blocks = s // Q_BLOCK
    kpos = jnp.arange(s)
    bi = jnp.arange(b)[:, None, None]
    iwf = iw.astype(jnp.float32) * IDX_HEADS ** -0.5

    def block(i):
        start = i * Q_BLOCK
        qb = lax.dynamic_slice_in_dim(q, start, Q_BLOCK, axis=2)
        iqb = lax.dynamic_slice_in_dim(iq, start, Q_BLOCK, axis=2)
        iwb = lax.dynamic_slice_in_dim(iwf, start, Q_BLOCK, axis=1)
        qpos = start + jnp.arange(Q_BLOCK)
        logits = jnp.einsum('bhqd,bsd->bhqs', iqb, ik).astype(jnp.float32) * IDX_DIM ** -0.5
        score = jnp.einsum('bhqs,bqh->bqs', jax.nn.relu(logits), iwb)
        score = jnp.where((kpos[None, :] <= qpos[:, None])[None], score, -jnp.inf)
        _, idx = lax.top_k(score, topk)
        kg = k[bi, idx]
        vg = v[bi, idx]
        valid = idx <= qpos[None, :, None]
        sc = jnp.einsum('bhqd,bqkd->bhqk', qb, kg).astype(jnp.float32) * ATTN_SCALE
        p = jax.nn.softmax(jnp.where(valid[:, None], sc, -jnp.inf), axis=-1)
        return jnp.einsum('bhqk,bqkd->bhqd', p, vg.astype(jnp.float32))

    o = lax.map(block, jnp.arange(n_blocks))
    return o.transpose(1, 2, 0, 3, 4).reshape(b, ha, s, dh)

def compress_blocks(x, pe, w1, w2):
    b, g, s, dh = x.shape
    ratio = CMP_BLOCK // CMP_STRIDE
    chunks = x.reshape(b, g, s // CMP_STRIDE, CMP_STRIDE, dh)
    n_cmp = s // CMP_STRIDE - ratio + 1
    blocks = jnp.concatenate([chunks[:, :, j:j + n_cmp] for j in range(ratio)], axis=3)
    flat = (blocks + pe).reshape(b, g, n_cmp, CMP_BLOCK * dh)
    return jax.nn.gelu(flat @ w1) @ w2

def selected_block_attention(q, k, v, sel):
    b, g, r, s, dh = q.shape
    n_sel = sel.shape[-1]
    n_chunk = s // SEL_Q_CHUNK
    kb = k.reshape(b, g, s // SEL_BLOCK, SEL_BLOCK, dh)
    vb = v.reshape(b, g, s // SEL_BLOCK, SEL_BLOCK, dh)
    qc = q.reshape(b, g, r, n_chunk, SEL_Q_CHUNK, dh).transpose(3, 0, 1, 2, 4, 5)
    selc = sel.reshape(b, g, n_chunk, SEL_Q_CHUNK, n_sel).transpose(2, 0, 1, 3, 4)
    bi = jnp.arange(b)[:, None, None, None]
    gi = jnp.arange(g)[None, :, None, None]
    offs = jnp.arange(SEL_BLOCK)

    def chunk(args):
        qx, sx, ci = args
        kg = kb[bi, gi, sx].reshape(b, g, SEL_Q_CHUNK, n_sel * SEL_BLOCK, dh)
        vg = vb[bi, gi, sx].reshape(b, g, SEL_Q_CHUNK, n_sel * SEL_BLOCK, dh)
        kpos = (sx[..., None] * SEL_BLOCK + offs).reshape(b, g, SEL_Q_CHUNK, n_sel * SEL_BLOCK)
        qpos = ci * SEL_Q_CHUNK + jnp.arange(SEL_Q_CHUNK)
        valid = kpos <= qpos[None, None, :, None]
        sc = jnp.einsum('bgrqd,bgqkd->bgrqk', qx, kg).astype(jnp.float32) * ATTN_SCALE
        p = jax.nn.softmax(jnp.where(valid[:, :, None], sc, -jnp.inf), axis=-1)
        return jnp.einsum('bgrqk,bgqkd->bgrqd', p, vg.astype(jnp.float32))

    o = lax.map(chunk, (qc, selc, jnp.arange(n_chunk)))
    return o.transpose(1, 2, 3, 0, 4, 5).reshape(b, g, r, s, dh)

def nsa_attention(q, k_cmp, v_cmp, k_slc, v_slc, k_win, v_win, gate_logits, cos, sin,
                  pe_k, w1_k, w2_k, pe_v, w1_v, w2_v):
    b, hc, s, dh = q.shape
    g, r = C_KV_GROUPS, C_GROUP_SIZE
    qg = q.reshape(b, g, r, s, dh)
    t = jnp.arange(s)

    kc = compress_blocks(k_cmp, pe_k, w1_k, w2_k)
    vc = compress_blocks(v_cmp, pe_v, w1_v, w2_v)
    n_cmp = kc.shape[2]
    sc = jnp.einsum('bgrsd,bgcd->bgrsc', qg, kc).astype(jnp.float32) * ATTN_SCALE
    cmp_end = jnp.arange(n_cmp) * CMP_STRIDE + CMP_BLOCK - 1
    cmask = cmp_end[None, :] <= t[:, None]
    sc = jnp.where(cmask, sc, -jnp.inf)
    mx = jnp.max(sc, axis=-1, keepdims=True)
    mx = jnp.where(jnp.isfinite(mx), mx, 0.0)
    e = jnp.where(cmask, jnp.exp(sc - mx), 0.0)
    den = jnp.sum(e, axis=-1, keepdims=True)
    p_cmp = e / jnp.where(den > 0, den, 1.0)
    o_cmp = jnp.einsum('bgrsc,bgcd->bgrsd', p_cmp, vc.astype(jnp.float32))

    n_slc = s // SEL_BLOCK
    c_start = np.arange(n_cmp) * CMP_STRIDE
    n_start = np.arange(n_slc) * SEL_BLOCK
    intersect = ((c_start[:, None] < n_start[None, :] + SEL_BLOCK)
                 & (c_start[:, None] + CMP_BLOCK > n_start[None, :])).astype(np.float32)
    imp = jnp.einsum('bgrsc,cn->bgsn', p_cmp, jnp.asarray(intersect))
    blk = jnp.arange(n_slc)[None, :]
    cur = (t // SEL_BLOCK)[:, None]
    admissible = blk <= cur
    forced = (blk == 0) | (blk == cur) | (blk == cur - 1)
    imp = jnp.where(admissible, jnp.where(forced, jnp.inf, imp), -jnp.inf)
    _, sel = lax.top_k(imp, min(SEL_COUNT, n_slc))
    qr = apply_rope(qg, cos, sin)
    o_slc = selected_block_attention(qr, apply_rope(k_slc, cos, sin), v_slc, sel)

    o_win, _ = banded_attention(qr.reshape(b * g, r, s, dh),
                                apply_rope(k_win, cos, sin).reshape(b * g, s, dh),
                                v_win.reshape(b * g, s, dh), WIN_SIZE - 1, BAND_BLOCK)
    o_win = o_win.reshape(b, g, r, s, dh)

    gates = jax.nn.sigmoid(gate_logits.astype(jnp.float32)).reshape(b, s, g, r, 3)
    gates = gates.transpose(4, 0, 2, 3, 1)[..., None]
    o = gates[0] * o_cmp + gates[1] * o_slc + gates[2] * o_win
    return o.reshape(b, hc, s, dh)

def setup_inputs(seed: int = 0) -> dict:
    key = jax.random.key(seed)
    ks = jax.random.split(key, 16)
    f32 = jnp.float32

    def nrm(k, shape, fan_in):
        return jax.random.normal(k, shape, f32) * fan_in ** -0.5

    def gain(k):
        return 1.0 + 0.05 * jax.random.normal(k, (DEPTH, D_MODEL), f32)

    flat_cmp = CMP_BLOCK * HEAD_DIM
    mix_width = N_HEADS * HEAD_DIM
    return {
        'x': jax.random.normal(ks[0], (BATCH, SEQ, D_MODEL), f32),
        'w_in': nrm(ks[1], (DEPTH, D_MODEL, IN_WIDTH), D_MODEL),
        'w_out': nrm(ks[2], (DEPTH, mix_width, D_MODEL), mix_width),
        'cmp_pe_k': 0.1 * jax.random.normal(ks[3], (DEPTH, CMP_BLOCK, HEAD_DIM), f32),
        'cmp_w1_k': nrm(ks[4], (DEPTH, flat_cmp, CMP_HIDDEN), flat_cmp),
        'cmp_w2_k': nrm(ks[5], (DEPTH, CMP_HIDDEN, HEAD_DIM), CMP_HIDDEN),
        'cmp_pe_v': 0.1 * jax.random.normal(ks[6], (DEPTH, CMP_BLOCK, HEAD_DIM), f32),
        'cmp_w1_v': nrm(ks[7], (DEPTH, flat_cmp, CMP_HIDDEN), flat_cmp),
        'cmp_w2_v': nrm(ks[8], (DEPTH, CMP_HIDDEN, HEAD_DIM), CMP_HIDDEN),
        'w_gate': nrm(ks[9], (DEPTH, D_MODEL, D_FF), D_MODEL),
        'w_up': nrm(ks[10], (DEPTH, D_MODEL, D_FF), D_MODEL),
        'w_down': nrm(ks[11], (DEPTH, D_FF, D_MODEL), D_FF),
        'g_pre_mix': gain(ks[12]),
        'g_post_mix': gain(ks[13]),
        'g_pre_ffn': gain(ks[14]),
        'g_post_ffn': gain(ks[15]),
    }

def reference(x, w_in, w_out, cmp_pe_k, cmp_w1_k, cmp_w2_k, cmp_pe_v, cmp_w1_v, cmp_w2_v,
              w_gate, w_up, w_down, g_pre_mix, g_post_mix, g_pre_ffn, g_post_ffn):
    b, s, _ = x.shape
    cos, sin = rope_tables(s, HEAD_DIM)
    icos, isin = rope_tables(s, IDX_DIM)
    splits = [int(v) for v in np.cumsum(IN_WIDTHS)[:-1]]

    def heads(t, n):
        return t.reshape(b, s, n, -1).transpose(0, 2, 1, 3)

    def merge(o):
        return o.transpose(0, 2, 1, 3).reshape(b, s, -1)

    for layer in range(DEPTH):
        h = rms_norm(x, g_pre_mix[layer])
        (a_q, a_k, a_v, i_q, i_k, i_w, b_q, b_k, b_v, c_q,
         c_kc, c_vc, c_ks, c_vs, c_kw, c_vw, c_g) = jnp.split(h @ w_in[layer], splits, axis=-1)

        o_a = dsa_attention(apply_rope(heads(a_q, A_HEADS), cos, sin),
                            apply_rope(a_k, cos, sin), a_v,
                            apply_rope(heads(i_q, IDX_HEADS), icos, isin),
                            apply_rope(i_k, icos, isin), i_w)
        o_b = dilated_mixture(apply_rope(heads(b_q, B_HEADS), cos, sin),
                              apply_rope(heads(b_k, B_HEADS), cos, sin),
                              heads(b_v, B_HEADS))
        o_c = nsa_attention(heads(c_q, C_HEADS),
                            heads(c_kc, C_KV_GROUPS), heads(c_vc, C_KV_GROUPS),
                            heads(c_ks, C_KV_GROUPS), heads(c_vs, C_KV_GROUPS),
                            heads(c_kw, C_KV_GROUPS), heads(c_vw, C_KV_GROUPS),
                            c_g, cos, sin,
                            cmp_pe_k[layer], cmp_w1_k[layer], cmp_w2_k[layer],
                            cmp_pe_v[layer], cmp_w1_v[layer], cmp_w2_v[layer])

        mixed = jnp.concatenate([merge(o_a), merge(o_b), merge(o_c)], axis=-1).astype(x.dtype)
        x = x + rms_norm(mixed @ w_out[layer], g_post_mix[layer])

        h = rms_norm(x, g_pre_ffn[layer])
        f = (jax.nn.silu(h @ w_gate[layer]) * (h @ w_up[layer])) @ w_down[layer]
        x = x + rms_norm(f, g_post_ffn[layer])
    return x


_drawn_inputs = setup_inputs


def setup_inputs(seed=0):
    import zlib

    import numpy as np

    out = dict(_drawn_inputs(seed))
    spreads = {}
    factors = {'cmp_pe_k': 2.886}
    for name, (base, spread) in spreads.items():
        noise = np.random.default_rng([zlib.crc32(name.encode()), seed]).standard_normal(out[name].shape)
        drawn = base * np.exp(spread * noise) if base else spread * noise
        out[name] = jnp.asarray(drawn.astype(out[name].dtype))
    for name, factor in factors.items():
        out[name] = (out[name] * factor).astype(out[name].dtype)
    return out
```

```python
from contextlib import ExitStack

import concourse.bass as bass
from concourse import mybir

F32 = mybir.dt.float32
F32R = mybir.dt.float32r
BF16 = mybir.dt.bfloat16
ACT = mybir.ActivationFunctionType
ALU = mybir.AluOpType
AX = mybir.AxisListType

P = 128
SEQ = 256
NT = SEQ // P
D = 2048
KC = D // P
DEPTH = 2
HD = 128
A_HEADS, B_HEADS, C_HEADS = 4, 4, 8
IDX_HEADS, IDX_DIM = 16, 64
TOPK = 64
D_FF = 5632
SCALE = HD ** -0.5
EPS = 1e-6
CMP_BLOCK, CMP_STRIDE, CMP_HIDDEN = 32, 16, 256
N_CMP = SEQ // CMP_STRIDE - 1
GROUPS = 2
NEG = -1.0e30
TAKEN = -3.0e38

A_Q = 0
A_K = A_Q + A_HEADS * HD
A_V = A_K + HD
I_Q = A_V + HD
I_K = I_Q + IDX_HEADS * IDX_DIM
I_W = I_K + IDX_DIM
B_Q = I_W + IDX_HEADS
B_K = B_Q + B_HEADS * HD
B_V = B_K + B_HEADS * HD
C_Q = B_V + B_HEADS * HD
C_KC = C_Q + C_HEADS * HD
C_VC = C_KC + GROUPS * HD
C_KS = C_VC + GROUPS * HD
C_VS = C_KS + GROUPS * HD
C_KW = C_VS + GROUPS * HD
C_VW = C_KW + GROUPS * HD
C_G = C_VW + GROUPS * HD
IN_W = C_G + 3 * C_HEADS

IN_BLOCKS = 14
IN_N = IN_W // IN_BLOCKS
N = 512
OUT_BLOCKS = D // N
FF_BLOCKS = D_FF // N
FF_KC = D_FF // P

RING = 4
CPB = KC // 2
IN_0 = 0
W1_0 = IN_0 + IN_BLOCKS * CPB
W1_CHUNKS = 16
OUT_0 = W1_0 + W1_CHUNKS
FF_0 = OUT_0 + OUT_BLOCKS * CPB
DN_0 = FF_0 + FF_BLOCKS * 2 * CPB
DN_CHUNKS = FF_KC // 2

T_CQR, T_KS, T_KW, T_CQ, T_AQ, T_AK, T_BQ, T_BK, T_IQ, T_IK = 0, 8, 10, 12, 20, 24, 25, 29, 33, 41
T_SLOTS = 42

K_ID = 0
K_CAUSAL = K_ID + P
K_DIL = K_CAUSAL + 3 * P
K_CBIAS = K_DIL + 3 * P
K_CKEEP = K_CBIAS + NT * N_CMP
K_NONE = K_CKEEP + NT * N_CMP
K_COS = K_NONE + NT
K_SIN = K_COS + NT * 64
K_ICOS = K_SIN + NT * 64
K_ISIN = K_ICOS + NT * 32
K_END = K_ISIN + NT * 32


def constants():
    import numpy as np

    out = np.zeros((P, K_END), np.float32)
    out[:, K_ID:K_ID + P] = np.eye(P, dtype=np.float32)
    t = np.arange(SEQ)[:, None]
    s = np.arange(SEQ)[None, :]

    def slab(full):
        return np.concatenate([full[P:, :], full[:P, :P]], axis=1)

    out[:, K_CAUSAL:K_CAUSAL + 3 * P] = slab(np.where(s <= t, 0.0, NEG))
    count = sum(((t - s >= 0) & (t - s <= w) & ((t - s) % d == 0)).astype(np.int64)
                for w, d in ((128, 1), (512, 4), (2048, 16)))
    out[:, K_DIL:K_DIL + 3 * P] = slab(np.where(count > 0, np.log(np.maximum(count, 1)) / SCALE, NEG))
    ends = np.arange(N_CMP) * CMP_STRIDE + CMP_BLOCK - 1
    seen = ends[None, :] <= t
    for i in range(NT):
        rows = seen[i * P:(i + 1) * P]
        out[:, K_CBIAS + i * N_CMP:K_CBIAS + (i + 1) * N_CMP] = np.where(rows, 0.0, NEG)
        out[:, K_CKEEP + i * N_CMP:K_CKEEP + (i + 1) * N_CMP] = rows
        out[:, K_NONE + i] = ~rows.any(axis=1)
        for at_c, at_s, half in ((K_COS, K_SIN, 64), (K_ICOS, K_ISIN, 32)):
            dim = 2 * half
            inv = np.float32(1.0) / (np.float32(10000.0) ** (np.arange(0, dim, 2, dtype=np.float32) / np.float32(dim)))
            angle = np.arange(i * P, (i + 1) * P, dtype=np.float32)[:, None] * inv[None, :].astype(np.float32)
            out[:, at_c + i * half:at_c + (i + 1) * half] = np.cos(angle)
            out[:, at_s + i * half:at_s + (i + 1) * half] = np.sin(angle)
    return out


def hybrid_trunk(nc, x, w_in, w_out, pe_k, w1_k, w2_k, pe_v, w1_v, w2_v, w_gate, w_up, w_down,
                 g_pre_mix, g_post_mix, g_pre_ffn, g_post_ffn, consts, out):
    with ExitStack() as ctx:
        def sb(name, shape, dt=F32, where=ctx):
            return where.enter_context(nc.sbuf_tensor(name, shape, dt))

        X = sb("X", [P, NT, D])
        raw = sb("raw", [P, RING, 2 * N])
        KON = sb("KON", [P, K_END])
        ident_b = sb("ident_b", [P, P], BF16)
        causal_b = sb("causal_b", [P, 3 * P], BF16)
        topk_b = sb("topk_b", [P, 3 * P], BF16)
        gain_rows = sb("gain_rows", [4 * KC, P])
        gain_all = sb("gain_all", [P, 4 * KC])
        gain = sb("gain", [P, 2, KC])
        pe_rows = sb("pe_rows", [2 * CMP_BLOCK, P])
        pe_T = sb("pe_T", [P, 2, CMP_BLOCK])
        w2 = sb("w2", [P, 2, 2, HD])
        hid_v = sb("hid_v", [P, 2, GROUPS, 4, 32])
        p_cmp = sb("p_cmp", [P, NT, C_HEADS, 32])
        stat = sb("stat", [P, 16])
        ss_part = sb("ss_part", [P, NT, OUT_BLOCKS])

        with ExitStack() as s1:
            actT_hi = sb("actT_hi", [P, KC, SEQ], F32R, s1)
            actT_lo = sb("actT_lo", [P, KC, SEQ], F32R, s1)
        with ExitStack() as s1:
            Y_ffn = sb("Y_ffn", [P, NT, D], F32, s1)
            gb_ffn = sb("gb_ffn", [P, D], F32, s1)
            sq_ffn = sb("sq_ffn", [P, NT, N], F32, s1)
        sb("place_act", [P, 2 * KC * SEQ])

        with ExitStack() as s1:
            w_hi = sb("w_hi", [P, RING, 2 * N], F32R, s1)
            w_lo = sb("w_lo", [P, RING, 2 * N], F32R, s1)
        with ExitStack() as s1:
            kvT = sb("kvT", [P, 2, GROUPS, SEQ], F32, s1)
            blk = sb("blk", [P, 2, CMP_BLOCK, GROUPS, N_CMP], F32, s1)
            relu = sb("relu", [P, 3, N], F32, s1)
            E = sb("E", [P, 3, 3 * P], F32, s1)
            PT = sb("PT", [P, 2, 3 * P], F32, s1)
            hid_k = sb("hid_k", [P, 2, GROUPS * N_CMP], F32, s1)
            kcT = sb("kcT", [P, GROUPS * N_CMP], F32, s1)
            vc = sb("vc", [P, GROUPS, HD], F32, s1)
            sc = sb("sc", [P, NT, C_HEADS, N_CMP], F32, s1)
            pcT = sb("pcT", [P, GROUPS, SEQ], F32, s1)
            gate = sb("gate", [P, NT, C_HEADS, 3], F32, s1)
            small = sb("small", [P, 96], F32, s1)
        sb("place_split", [P, 2 * RING * 2 * N])

        with ExitStack() as s1:
            rows = sb("rows", [P, NT, IN_W], F32, s1)
            QT = sb("QT", [P, T_SLOTS, SEQ], F32, s1)
            rt = sb("rt", [P, 4, 256], F32, s1)
            ik2 = sb("ik2", [P, NT, 2 * IDX_DIM], F32, s1)
            acc = sb("acc", [P, 3 * P], F32, s1)
            work = sb("work", [P, 3 * P], F32, s1)
        with ExitStack() as s1:
            sb("under_cqr", [P, NT * IN_W + T_IQ * SEQ + SEQ], F32, s1)
            cqr = sb("cqr", [P, NT, C_HEADS * HD], F32, s1)
        with ExitStack() as s1:
            Y_mix = sb("Y_mix", [P, NT, D], F32, s1)
            xn = sb("xn", [P, NT, D], F32, s1)
            gb_mix = sb("gb_mix", [P, D], F32, s1)
            sq_mix = sb("sq_mix", [P, NT, N], F32, s1)
        with ExitStack() as s1:
            hT_hi = sb("hT_hi", [P, FF_KC, SEQ], F32R, s1)
            hT_lo = sb("hT_lo", [P, FF_KC, SEQ], F32R, s1)
            hrow = sb("hrow", [P, NT, N], F32, s1)

        bank = [ctx.enter_context(nc.psum_tensor(f"bank{i}", [P, N], F32)) for i in range(8)]
        ident = KON[:, K_ID:K_ID + P]
        causal = KON[:, K_CAUSAL:K_CAUSAL + 3 * P]
        dilated = KON[:, K_DIL:K_DIL + 3 * P]

        sems = []

        def sem(name):
            sems.append(ctx.enter_context(nc.semaphore(name)))
            return sems[-1]

        loaded = sem("loaded")
        cast = sem("cast")
        gains_T = sem("gains_T")
        raw_in = [sem(f"raw_in{i}") for i in range(RING)]
        hi_done = sem("hi_done")
        lo_done = sem("lo_done")
        mm_done = sem("mm_done")
        sq_done = sem("sq_done")
        ysq_done = sem("ysq_done")
        ms_ready = sem("ms_ready")
        sd_ready = sem("sd_ready")
        xn_ready = sem("xn_ready")
        nt_ready = sem("nt_ready")
        nt_hi = sem("nt_hi")
        nt_lo = sem("nt_lo")
        x_new = sem("x_new")
        gain_ready = sem("gain_ready")
        ev_a = sem("ev_a")
        ev_v = sem("ev_v")
        rot = sem("rot")
        roped = sem("roped")
        pe_in = sem("pe_in")
        w2_in = sem("w2_in")
        gb_in = sem("gb_in")
        qt_ready = sem("qt_ready")
        qt_a = sem("qt_a")
        qt_v = sem("qt_v")
        pe_t = sem("pe_t")
        lg_ready = sem("lg_ready")
        relu_done = sem("relu_done")
        acc_done = sem("acc_done")
        topk_done = sem("topk_done")
        blk_done = sem("blk_done")
        gelu_done = sem("gelu_done")
        kv_ready = sem("kv_ready")
        kv_ev = sem("kv_ev")
        csc_ready = sem("csc_ready")
        csub = sem("csub")
        cexp = sem("cexp")
        pc_ready = sem("pc_ready")
        pct_ready = sem("pct_ready")
        pct_ev = sem("pct_ev")
        gexp = sem("gexp")
        s_ready = sem("s_ready")
        max_done = sem("max_done")
        exp_done = sem("exp_done")
        scaled = sem("scaled")
        t_ready = sem("t_ready")
        pt_a = sem("pt_a")
        pt_v = sem("pt_v")
        o_ready = sem("o_ready")
        o_hi = sem("o_hi")
        o_lo = sem("o_lo")
        y_ev = sem("y_ev")
        silu_done = sem("silu_done")
        h_ready = sem("h_ready")
        ht_ready = sem("ht_ready")
        ht_hi = sem("ht_hi")
        ht_lo = sem("ht_lo")
        chain = sem("chain")
        x_out = sem("x_out")

        PIECES = [(A_Q, 4, HD), (A_K, 1, HD), (I_Q, 8, IDX_DIM), (I_Q + 512, 8, IDX_DIM), (I_K, 1, IDX_DIM),
                  (B_Q, 4, HD), (B_K, 4, HD), (C_Q, 4, HD), (C_Q + 512, 4, HD), (C_KS, 2, HD), (C_KW, 2, HD)]

        def row_cols(col):
            return lambda t: rows[:, t, col:col + P]

        TILES = [(lambda t, h=h: cqr[:, t, h * HD:(h + 1) * HD], QT[:, T_CQR + h, :]) for h in range(C_HEADS)]
        TILES += [(row_cols(C_KC + g * HD), kvT[:, 0, g, :]) for g in range(GROUPS)]
        TILES += [(row_cols(C_VC + g * HD), kvT[:, 1, g, :]) for g in range(GROUPS)]
        TILES += [(row_cols(I_Q + i * P), QT[:, T_IQ + i, :]) for i in range(8)]
        TILES += [(row_cols(A_K), QT[:, T_AK, :]), (lambda t: ik2[:, t, :], QT[:, T_IK, :])]
        TILES += [(row_cols(C_KS + g * HD), QT[:, T_KS + g, :]) for g in range(GROUPS)]
        TILES += [(row_cols(C_KW + g * HD), QT[:, T_KW + g, :]) for g in range(GROUPS)]
        TILES += [(row_cols(C_Q + h * HD), QT[:, T_CQ + h, :]) for h in range(C_HEADS)]
        TILES += [(row_cols(A_Q + h * HD), QT[:, T_AQ + h, :]) for h in range(A_HEADS)]
        TILES += [(row_cols(B_Q + h * HD), QT[:, T_BQ + h, :]) for h in range(B_HEADS)]
        TILES += [(row_cols(B_K + h * HD), QT[:, T_BK + h, :]) for h in range(B_HEADS)]
        PAIRS = len(TILES) // 2

        LOGITS = [(1, [4 * g + odd, 4 * g + 2 + odd]) for g in range(4) for odd in range(2)]
        LOGITS += [(0, [8 * g + 2 * j + odd for j in range(4)]) for g in range(2) for odd in range(2)]

        UNITS = [(T_BQ + h, T_BK + h, B_V + h * HD, "dilated", A_HEADS + h, True, True, None)
                 for h in range(B_HEADS)]
        UNITS += [(T_AQ + h, T_AK, A_V, "topk", h, True, True, None) for h in range(A_HEADS)]
        for h in range(C_HEADS):
            g = h // 4
            o = A_HEADS + B_HEADS + h
            UNITS += [(T_CQR + h, T_KS + g, C_VS + g * HD, "causal", o, True, False, 1),
                      (T_CQR + h, T_KW + g, C_VW + g * HD, "causal", o, False, True, 2)]
        NU = len(UNITS)
        HEADS_DONE = []
        done = 0
        for u in UNITS:
            done += u[6]
            HEADS_DONE.append(done)

        def chunk_view(buf, slot, n):
            return buf[:, slot, 0:2 * n].rearrange("p (c n) -> p c n", c=2)

        with nc.Block() as block:
            @block.sync
            def _(sp):
                sp.dma_start(KON[:], consts).then_inc(loaded, 16)
                sp.dma_start(X[:], x[0].rearrange("(t p) d -> p t d", p=P)).then_inc(loaded, 16)
                for i, g in enumerate((g_pre_mix, g_pre_ffn)):
                    sp.dma_start(gain_rows[i * DEPTH * KC:(i + 1) * DEPTH * KC, :],
                                 g.rearrange("l (c p) -> (l c) p", p=P)).then_inc(loaded, 16)

            @block.gpsimd
            def _(pool):
                nc.gpsimd.memset(hid_v[:], 0.0)
                nc.gpsimd.memset(p_cmp[:], 0.0)

            @block.vector
            def _(dve):
                dve.wait_ge(loaded, 64)
                nc.vector.tensor_copy(ident_b[:], ident)
                nc.vector.tensor_copy(causal_b[:], causal)
                dve.wait_ge(gains_T, 1)
                nc.vector.tensor_copy(gain_all[:], bank[0][:, 0:4 * KC])

            @block.tensor
            def _(pe):
                pe.wait_ge(loaded, 64)
                nc.tensor.transpose(bank[0][:, 0:4 * KC], gain_rows[:, :],
                                    ident[0:4 * KC, 0:4 * KC]).then_inc(gains_T, 1)
        nc.gpsimd.sem_clear(range(sems[0].num, sems[-1].num + 1))
        nc.all_engine_barrier()

        with nc.Fori(0, DEPTH) as layer:
            with nc.Block() as block:

                @block.sync
                def _(sp):
                    def w_chunk(w, row, col, n):
                        return w[bass.ds(layer, 1), row:row + 2 * P, bass.ds(col, n)].rearrange(
                            "l (c p) n -> p (l c) n", p=P)

                    def load(i, src, n):
                        sp.dma_start(chunk_view(raw, i % RING, n), src).then_inc(raw_in[i % RING], 16)

                    sp.dma_start(pe_rows[0:CMP_BLOCK, :], pe_k[bass.ds(layer, 1)].rearrange("l j d -> (l j) d")
                                 ).then_inc(pe_in, 16)
                    sp.dma_start(pe_rows[CMP_BLOCK:, :], pe_v[bass.ds(layer, 1)].rearrange("l j d -> (l j) d")
                                 ).then_inc(pe_in, 16)
                    for kv, w in enumerate((w2_k, w2_v)):
                        sp.dma_start(w2[:, kv], w[bass.ds(layer, 1)].rearrange("l (h p) d -> p (l h) d", p=P)
                                     ).then_inc(w2_in, 16)

                    for i in range(2 * CPB):
                        if i >= RING:
                            sp.wait_ge(lo_done, i - RING + 1)
                        load(i, w_chunk(w_in, (i % CPB) * 2 * P, (i // CPB) * IN_N, IN_N), IN_N)
                    with sp.Fori(1, IN_BLOCKS // 2) as it:
                        for i in range(2 * CPB):
                            sp.wait_ge(lo_done, 2 * CPB * it + (i - RING + 1))
                            load(i, w_chunk(w_in, (i % CPB) * 2 * P, (2 * it + i // CPB) * IN_N, IN_N), IN_N)

                    for i in range(W1_CHUNKS):
                        if i < RING:
                            sp.wait_ge(lo_done, W1_0 + i - RING + 1)
                        else:
                            sp.wait_ge(mm_done, W1_0 + i - RING + 1)
                        w = (w1_k, w1_v)[i // 8]
                        j = (i % 8) * 4
                        sp.dma_start(raw[:, i % RING, :].rearrange("p (j h) -> p j h", j=4),
                                     w[bass.ds(layer, 1), j * HD:(j + 4) * HD, :].rearrange(
                                         "l (j d) h -> d (l j) h", d=HD)).then_inc(raw_in[i % RING], 16)

                    for i in range(RING):
                        sp.wait_ge(mm_done, OUT_0 + i - RING + 1)
                        load(i, w_chunk(w_out, i * 2 * P, 0, N), N)
                    for i in range(RING, 2 * CPB):
                        sp.wait_ge(lo_done, OUT_0 - W1_CHUNKS + i - RING + 1)
                        load(i, w_chunk(w_out, (i % CPB) * 2 * P, (i // CPB) * N, N), N)
                    for i in range(2 * CPB):
                        sp.wait_ge(lo_done, OUT_0 - W1_CHUNKS + 2 * CPB + i - RING + 1)
                        load(i, w_chunk(w_out, (i % CPB) * 2 * P, (2 + i // CPB) * N, N), N)
                    sp.dma_start(gb_mix[:], g_post_mix[bass.ds(layer, 1), :].partition_broadcast(P)
                                 ).then_inc(gb_in, 16)

                    with sp.Fori(0, FF_BLOCKS) as j:
                        for i in range(2 * CPB):
                            sp.wait_ge(lo_done, 2 * CPB * j + (FF_0 - W1_CHUNKS + i - RING + 1))
                            load(i, w_chunk(w_gate if i < CPB else w_up, (i % CPB) * 2 * P, j * N, N), N)

                    with sp.Fori(0, OUT_BLOCKS // 2) as it:
                        for i in range(2 * DN_CHUNKS):
                            sp.wait_ge(lo_done, 2 * DN_CHUNKS * it + (DN_0 - W1_CHUNKS + i - RING + 1))
                            load(i, w_chunk(w_down, (i % DN_CHUNKS) * 2 * P, (2 * it + i // DN_CHUNKS) * N, N), N)
                    sp.dma_start(gb_ffn[:], g_post_ffn[bass.ds(layer, 1), :].partition_broadcast(P)
                                 ).then_inc(gb_in, 16)

                @block.gpsimd
                def _(pool):
                    steps = 0
                    for k, (col, heads, width) in enumerate(PIECES):
                        half = width // 2
                        block_done = (col + heads * width - 1) // IN_N + 1
                        pool.wait_ge(ev_a, block_done)
                        pool.wait_ge(ev_v, block_done)
                        at_c, at_s = (K_COS, K_SIN) if width == HD else (K_ICOS, K_ISIN)
                        for t in range(NT):
                            src = rows[:, t, col:col + heads * width].rearrange("p (h w) -> p h w", w=width)
                            x1, x2 = src[:, :, 0:half], src[:, :, half:width]
                            cos = KON[:, None, at_c + t * half:at_c + (t + 1) * half].to_broadcast([P, heads, half])
                            sin = KON[:, None, at_s + t * half:at_s + (t + 1) * half].to_broadcast([P, heads, half])
                            tmp = [rt[:, i, 0:heads * half].rearrange("p (h w) -> p h w", w=half) for i in range(4)]
                            if steps:
                                pool.wait_ge(rot, steps)
                            nc.gpsimd.tensor_tensor(tmp[0], x1, cos, ALU.mult)
                            nc.gpsimd.tensor_tensor(tmp[1], x2, sin, ALU.mult)
                            nc.gpsimd.tensor_tensor(tmp[2], x2, cos, ALU.mult)
                            nc.gpsimd.tensor_tensor(tmp[3], x1, sin, ALU.mult).then_inc(rot, 1)
                            steps += 1
                            pool.wait_ge(rot, steps)
                            if C_Q <= col < C_KC:
                                at = col - C_Q
                                dst = [cqr[:, t, at:at + heads * width].rearrange("p (h w) -> p h w", w=width)]
                            elif col == I_K:
                                dst = [ik2[:, t, c * width:(c + 1) * width].rearrange("p (h w) -> p h w", w=width)
                                       for c in range(2)]
                            else:
                                dst = [src]
                            for d in dst:
                                nc.gpsimd.tensor_tensor(d[:, :, 0:half], tmp[0], tmp[1], ALU.subtract)
                                last = nc.gpsimd.tensor_tensor(d[:, :, half:width], tmp[2], tmp[3], ALU.add)
                            last.then_inc(rot, 1)
                            steps += 1
                    pool.wait_ge(rot, steps)
                    nc.gpsimd.memset(small[:, 95:96], 0.0).then_inc(roped, 1)

                @block.scalar
                def _(act):
                    def hi(i, n, rounds):
                        act.wait_ge(raw_in[i % RING], rounds)
                        nc.scalar.activation(w_hi[:, i % RING, 0:2 * n], raw[:, i % RING, 0:2 * n],
                                             ACT.Copy).then_inc(hi_done, 1)

                    def norm_T(which, base):
                        for b in range(KC // 2):
                            act.wait_ge(nt_ready, base + b + 1)
                            for c in range(2):
                                k = 2 * b + c
                                last = nc.scalar.activation(actT_hi[:, k, :], bank[4 + b % 4][:, c * SEQ:(c + 1) * SEQ],
                                                            ACT.Copy, scale=gain[:, which, k:k + 1])
                            last.then_inc(nt_hi, 1)

                    def squares(base):
                        for t in range(NT):
                            if base:
                                act.wait_ge(x_new, t + 1)
                            nc.scalar.activation(xn[:, t, :], X[:, t, :], ACT.Square,
                                                 accum_out=stat[:, t:t + 1]).then_inc(sq_done, 1)

                    def root(k):
                        act.wait_ge(ms_ready, k)
                        nc.scalar.activation(stat[:, 4:6], stat[:, 2:4], ACT.Sqrt).then_inc(sd_ready, 1)

                    squares(0)
                    root(1)
                    act.wait_ge(gain_ready, 1)
                    norm_T(0, 0)

                    def in_evac(b):
                        act.wait_ge(mm_done, CPB * (b + 1))
                        nc.scalar.activation(rows[:, 0, bass.ds(b * IN_N, IN_N)], bank_of[0][:, 0:IN_N],
                                             ACT.Copy).then_inc(ev_a, 1)

                    for i in range(2 * CPB):
                        if i >= RING:
                            act.wait_ge(mm_done, i - RING + 1)
                        hi(i, IN_N, 16 * (i // RING + 1))
                        if i == CPB + 3:
                            bank_of = bank[0:2]
                            in_evac(0)
                    with act.Fori(1, IN_BLOCKS // 2) as it:
                        for i in range(2 * CPB):
                            act.wait_ge(mm_done, 2 * CPB * it + (i - RING + 1))
                            hi(i, IN_N, 16 * (2 * CPB // RING) * it + 16 * (i // RING + 1))
                            if i == 3:
                                bank_of = bank[2:4]
                                in_evac(2 * it - 1)
                            if i == CPB + 3:
                                bank_of = bank[0:2]
                                in_evac(2 * it)
                    bank_of = bank[2:4]
                    in_evac(IN_BLOCKS - 1)

                    act.wait_ge(ev_v, IN_BLOCKS)
                    act.wait_ge(qt_ready, 1)
                    act.wait_ge(ev_a, IN_BLOCKS)
                    nc.scalar.activation(gate[:].rearrange("p t h b -> p t (h b)"), rows[:, :, C_G:C_G + 3 * C_HEADS],
                                         ACT.Exp, scale=-1.0).then_inc(gexp, 1)

                    for k in range(0, PAIRS, 2):
                        act.wait_ge(qt_ready, k + 1)
                        for c in range(2):
                            last = nc.scalar.activation(TILES[2 * k + c][1], bank[4 + k % 4][:, c * SEQ:(c + 1) * SEQ],
                                                        ACT.Copy)
                        last.then_inc(qt_a, 1)

                    for k in range(len(LOGITS)):
                        act.wait_ge(lg_ready, k + 1)
                        if k >= 3:
                            act.wait_ge(acc_done, k - 2)
                        nc.scalar.activation(relu[:, k % 3, :], bank[k % 4][:], ACT.Relu,
                                             scale=IDX_DIM ** -0.5 * IDX_HEADS ** -0.5).then_inc(relu_done, 1)

                    act.wait_ge(mm_done, W1_0 + 8)
                    for half in range(2):
                        last = nc.scalar.activation(hid_k[:, half, :], bank[4 + half][:, 0:GROUPS * N_CMP],
                                                    ACT.Gelu_apprx_tanh)
                    last.then_inc(gelu_done, 1)
                    act.wait_ge(mm_done, W1_0 + 16)
                    for half in range(2):
                        for r in range(4):
                            last = nc.scalar.activation(
                                hid_v[:, half, :, r, 0:N_CMP],
                                bank[6 + half][:, 0:GROUPS * N_CMP].rearrange("p (g c) -> p g c", g=GROUPS),
                                ACT.Gelu_apprx_tanh)
                    last.then_inc(gelu_done, 1)
                    act.wait_ge(kv_ready, 1)
                    nc.scalar.activation(kcT[:], bank[4][:, 0:GROUPS * N_CMP], ACT.Copy)
                    nc.scalar.activation(vc[:].rearrange("p g d -> p (g d)"), bank[4][:, P:P + GROUPS * HD],
                                         ACT.Copy).then_inc(kv_ev, 1)
                    act.wait_ge(csub, 1)
                    nc.scalar.activation(sc[:], sc[:], ACT.Exp).then_inc(cexp, 1)
                    act.wait_ge(pct_ready, 1)
                    nc.scalar.activation(pcT[:].rearrange("p g t -> p (g t)"), bank[6][:], ACT.Copy).then_inc(pct_ev, 1)

                    for i in range(NU + 4):
                        if i < NU:
                            act.wait_ge(max_done, i + 1)
                            if i >= 3:
                                act.wait_ge(t_ready, i - 2)
                            m = 8 + 4 * (i % 4)
                            nc.scalar.activation(E[:, i % 3, 0:SEQ], bank[i % 3][:, 0:SEQ], ACT.Exp, scale=SCALE,
                                                 bias=small[:, m + 1:m + 2], accum_out=small[:, m + 3:m + 4])
                            nc.scalar.activation(E[:, i % 3, SEQ:], bank[i % 3][:, SEQ:3 * P], ACT.Exp, scale=SCALE,
                                                 bias=small[:, m:m + 1], accum_out=small[:, m + 2:m + 3]
                                                 ).then_inc(exp_done, 1)
                        k = i - 2
                        if 0 <= k < NU and k % 2 == 0:
                            act.wait_ge(t_ready, k + 1)
                            if k >= 2:
                                act.wait_ge(o_ready, k - 1)
                            nc.scalar.activation(PT[:, k % 2, :], bank[3 + k % 2][:, 0:3 * P], ACT.Copy).then_inc(pt_a, 1)
                        k = i - 4
                        if 0 <= k < NU and UNITS[k][6]:
                            act.wait_ge(o_ready, k + 1)
                            nc.scalar.activation(actT_hi[:, UNITS[k][4], :], bank[5 + HEADS_DONE[k] % 2][:, 0:SEQ],
                                                 ACT.Copy).then_inc(o_hi, 1)

                    def y_squares(Y, sq, b, base, first=False):
                        act.wait_ge(y_ev, base + b + 1)
                        if not first:
                            act.wait_ge(ysq_done, base + b)
                        for t in range(NT):
                            last = nc.scalar.activation(sq[:, t, :], Y[:, t, bass.ds(b * N, N)], ACT.Square,
                                                        accum_out=ss_part[:, t, bass.ds(b, 1)])
                        last.then_inc(ysq_done, 1)

                    act.wait_ge(o_lo, A_HEADS + B_HEADS + C_HEADS)
                    for i in range(4 * CPB):
                        if i == 0:
                            act.wait_ge(mm_done, OUT_0)
                        if i >= RING:
                            act.wait_ge(mm_done, OUT_0 + i - RING + 1)
                        hi(i, N, 16 * ((OUT_0 + i) // RING + 1))
                        if i % CPB == 5 and i > CPB:
                            y_squares(Y_mix, sq_mix, i // CPB - 1, 0, i // CPB == 1)
                    y_squares(Y_mix, sq_mix, OUT_BLOCKS - 1, 0)
                    root(2)
                    squares(1)
                    root(3)
                    norm_T(1, KC // 2)

                    def turn(j, first):
                        for i in range(2 * CPB):
                            act.wait_ge(mm_done, 2 * CPB * j + (FF_0 + i - RING + 1))
                            hi(i, N, 16 * (2 * CPB // RING) * j + 16 * ((FF_0 + i) // RING + 1))
                            if i == CPB + 3:
                                if not first:
                                    act.wait_ge(ht_ready, j)
                                    for c in range(2):
                                        last = nc.scalar.activation(
                                            hT_hi[:, bass.ds(4 * j - 4 + 2 * c, 2), :].rearrange("p c t -> p (c t)"),
                                            bank[4 + c][:], ACT.Copy)
                                    last.then_inc(ht_hi, 1)
                                for t in range(NT):
                                    last = nc.scalar.activation(hrow[:, t, :], bank[t][:], ACT.Silu)
                                last.then_inc(silu_done, 1)

                    turn(0, True)
                    with act.Fori(1, FF_BLOCKS) as j:
                        turn(j, False)
                    act.wait_ge(ht_ready, FF_BLOCKS)
                    for c in range(2):
                        last = nc.scalar.activation(
                            hT_hi[:, 4 * FF_BLOCKS - 4 + 2 * c:4 * FF_BLOCKS - 2 + 2 * c, :].rearrange("p c t -> p (c t)"),
                            bank[4 + c][:], ACT.Copy)
                    last.then_inc(ht_hi, 1)

                    with act.Fori(0, OUT_BLOCKS // 2) as it:
                        for i in range(2 * DN_CHUNKS):
                            act.wait_ge(mm_done, 2 * DN_CHUNKS * it + (DN_0 + i - RING + 1))
                            hi(i, N, 16 * (2 * DN_CHUNKS // RING) * it + 16 * ((DN_0 + i) // RING + 1))
                            if i == DN_CHUNKS + 5:
                                y_squares(Y_ffn, sq_ffn, 2 * it, OUT_BLOCKS)
                        y_squares(Y_ffn, sq_ffn, 2 * it + 1, OUT_BLOCKS)
                    root(4)

                @block.vector
                def _(dve):
                    steps = [0]

                    def link(ins):
                        steps[0] += 1
                        ins.then_inc(chain, 1)
                        dve.wait_ge(chain, steps[0])

                    def lo(i, n, count):
                        dve.wait_ge(hi_done, count)
                        s = i % RING
                        nc.vector.tensor_tensor(w_lo[:, s, 0:2 * n], raw[:, s, 0:2 * n],
                                                w_hi[:, s, 0:2 * n].bitcast(F32), ALU.subtract).then_inc(lo_done, 1)

                    def inverse_root(k):
                        nc.vector.tensor_scalar(stat[:, 2:4], stat[:, 0:2], 1.0 / D, EPS, ALU.mult, ALU.add
                                                ).then_inc(ms_ready, 1)
                        dve.wait_ge(sd_ready, k)
                        link(nc.vector.reciprocal(stat[:, 6:8], stat[:, 4:6]))
                        link(nc.vector.tensor_tensor(stat[:, 8:10], stat[:, 6:8], stat[:, 6:8], ALU.mult))
                        link(nc.vector.tensor_tensor(stat[:, 8:10], stat[:, 8:10], stat[:, 2:4], ALU.mult))
                        link(nc.vector.tensor_scalar(stat[:, 8:10], stat[:, 8:10], -0.5, 1.5, ALU.mult, ALU.add))
                        link(nc.vector.tensor_tensor(stat[:, 6:8], stat[:, 6:8], stat[:, 8:10], ALU.mult))

                    def norm_rows(k, squared):
                        dve.wait_ge(sq_done, squared)
                        inverse_root(k)
                        for t in range(NT):
                            nc.vector.tensor_scalar(xn[:, t, :], X[:, t, :], stat[:, 6 + t:7 + t], None, ALU.mult
                                                    ).then_inc(xn_ready, 1)

                    def norm_T(which, base):
                        for b in range(KC // 2):
                            dve.wait_ge(nt_hi, base + b + 1)
                            for c in range(2):
                                k = 2 * b + c
                                last = nc.vector.scalar_tensor_tensor(
                                    out=actT_lo[:, k, :], in0=bank[4 + b % 4][:, c * SEQ:(c + 1) * SEQ],
                                    scalar=gain[:, which, k:k + 1], in1=actT_hi[:, k, :].bitcast(F32),
                                    op0=ALU.mult, op1=ALU.subtract)
                            last.then_inc(nt_lo, 1)

                    nc.vector.tensor_copy(
                        gain[:], gain_all[:].rearrange("p (w l c) -> p w l c", w=2, l=DEPTH)[:, :, bass.ds(layer, 1), :]
                        .rearrange("p w l c -> p w (l c)")).then_inc(gain_ready, 1)
                    dve.wait_ge(gain_ready, 1)
                    norm_rows(1, NT)
                    norm_T(0, 0)

                    def in_evac(b, banks):
                        dve.wait_ge(mm_done, CPB * (b + 1))
                        nc.vector.tensor_copy(rows[:, 1, bass.ds(b * IN_N, IN_N)], banks[1][:, 0:IN_N]
                                              ).then_inc(ev_v, 1)

                    for i in range(2 * CPB):
                        lo(i, IN_N, i + 1)
                        if i == CPB + 3:
                            in_evac(0, bank[0:2])
                    with dve.Fori(1, IN_BLOCKS // 2) as it:
                        for i in range(2 * CPB):
                            lo(i, IN_N, 2 * CPB * it + i + 1)
                            if i == 3:
                                in_evac(2 * it - 1, bank[2:4])
                            if i == CPB + 3:
                                in_evac(2 * it, bank[0:2])
                    in_evac(IN_BLOCKS - 1, bank[2:4])

                    dve.wait_ge(pe_t, 1)
                    link(nc.vector.tensor_copy(pe_T[:].rearrange("p k j -> p (k j)"), bank[0][:, 0:2 * CMP_BLOCK]))
                    for k in range(1, PAIRS, 2):
                        dve.wait_ge(qt_ready, k + 1)
                        for c in range(2):
                            last = nc.vector.tensor_copy(TILES[2 * k + c][1], bank[4 + k % 4][:, c * SEQ:(c + 1) * SEQ])
                        last.then_inc(qt_v, 1)

                    dve.wait_ge(qt_a, PAIRS // 2 + 1)
                    dve.wait_ge(qt_v, PAIRS // 2)
                    for kv in range(2):
                        for g in range(GROUPS):
                            for h in range(2):
                                last = nc.vector.tensor_tensor(
                                    blk[:, kv, h * CMP_STRIDE:(h + 1) * CMP_STRIDE, g, :],
                                    kvT[:, kv, g, h * CMP_STRIDE:h * CMP_STRIDE + N_CMP * CMP_STRIDE].rearrange(
                                        "p (c j) -> p j c", j=CMP_STRIDE),
                                    pe_T[:, kv, h * CMP_STRIDE:(h + 1) * CMP_STRIDE].unsqueeze(2).to_broadcast(
                                        [P, CMP_STRIDE, N_CMP]), ALU.add)
                        last.then_inc(blk_done, 1)

                    started = {0: False, 1: False}
                    for k, (t, heads) in enumerate(LOGITS):
                        dve.wait_ge(relu_done, k + 1)
                        cols = slice(0, SEQ) if t else slice(SEQ, 3 * P)
                        width = SEQ if t else P
                        for n, h in enumerate(heads):
                            ins = nc.vector.scalar_tensor_tensor(
                                out=acc[:, cols], in0=relu[:, k % 3, n * width:(n + 1) * width],
                                scalar=rows[:, t, I_W + h:I_W + h + 1],
                                in1=acc[:, cols] if started[t] else causal[:, cols], op0=ALU.mult, op1=ALU.add)
                            started[t] = True
                            if n < len(heads) - 1:
                                link(ins)
                        ins.then_inc(acc_done, 1)
                        dve.wait_ge(acc_done, k + 1)

                    for r in range(TOPK // 8):
                        src = work if r else acc
                        nc.vector.max(small[:, 32:40], src[:, 0:SEQ])
                        link(nc.vector.max(small[:, 40:48], src[:, SEQ:]))
                        nc.vector.match_replace(work[:, 0:SEQ], small[:, 32:40], src[:, 0:SEQ], TAKEN)
                        link(nc.vector.match_replace(work[:, SEQ:], small[:, 40:48], src[:, SEQ:], TAKEN))
                    link(nc.vector.tensor_scalar(work[:], work[:], TAKEN, -1.0, ALU.is_equal, ALU.add))
                    nc.vector.scalar_tensor_tensor(out=topk_b[:], in0=work[:], scalar=-NEG, in1=causal,
                                                   op0=ALU.mult, op1=ALU.add).then_inc(topk_done, 1)

                    dve.wait_ge(gexp, 1)
                    link(nc.vector.tensor_scalar(gate[:], gate[:], 1.0, None, ALU.add))
                    link(nc.vector.reciprocal(gate[:], gate[:]))

                    dve.wait_ge(csc_ready, 1)
                    for t in range(NT):
                        ins = nc.vector.scalar_tensor_tensor(
                            out=sc[:, t], in0=bank[5][:, t * 120:(t + 1) * 120].rearrange("p (h c) -> p h c", c=N_CMP),
                            scalar=SCALE,
                            in1=KON[:, None, K_CBIAS + t * N_CMP:K_CBIAS + (t + 1) * N_CMP].to_broadcast(
                                [P, C_HEADS, N_CMP]), op0=ALU.mult, op1=ALU.add)
                    link(ins)
                    sc2 = sc[:].rearrange("p t h c -> p (t h) c")
                    link(nc.vector.tensor_reduce(small[:, 48:64], sc2, AX.X, ALU.max))
                    nc.vector.tensor_tensor(sc2, sc2, small[:, 48:64].unsqueeze(2).to_broadcast([P, 16, N_CMP]),
                                            ALU.subtract).then_inc(csub, 1)
                    dve.wait_ge(cexp, 1)
                    for t in range(NT):
                        ins = nc.vector.tensor_tensor(
                            sc[:, t], sc[:, t], KON[:, None, K_CKEEP + t * N_CMP:K_CKEEP + (t + 1) * N_CMP].to_broadcast(
                                [P, C_HEADS, N_CMP]), ALU.mult)
                    link(ins)
                    link(nc.vector.tensor_reduce(small[:, 64:80], sc2, AX.X, ALU.add))
                    for t in range(NT):
                        ins = nc.vector.tensor_scalar(small[:, 64 + 8 * t:72 + 8 * t], small[:, 64 + 8 * t:72 + 8 * t],
                                                      KON[:, K_NONE + t:K_NONE + t + 1], None, ALU.add)
                    link(ins)
                    link(nc.vector.reciprocal(small[:, 64:80], small[:, 64:80]))
                    link(nc.vector.tensor_tensor(small[:, 64:80], small[:, 64:80],
                                                 gate[:, :, :, 0].rearrange("p t h -> p (t h)"), ALU.mult))
                    nc.vector.tensor_tensor(p_cmp[:, :, :, 0:N_CMP].rearrange("p t h c -> p (t h) c"), sc2,
                                            small[:, 64:80].unsqueeze(2).to_broadcast([P, 16, N_CMP]), ALU.mult
                                            ).then_inc(pc_ready, 1)

                    for i in range(NU + 4):
                        if i < NU:
                            dve.wait_ge(s_ready, i + 1)
                            m = 8 + 4 * (i % 4)
                            nc.vector.tensor_reduce(small[:, m + 1:m + 2], bank[i % 3][:, 0:SEQ], AX.X, ALU.max,
                                                    negate=True)
                            link(nc.vector.tensor_reduce(small[:, m:m + 1], bank[i % 3][:, SEQ:3 * P], AX.X, ALU.max,
                                                         negate=True))
                            nc.vector.tensor_scalar(small[:, m:m + 2], small[:, m:m + 2], SCALE, None, ALU.mult
                                                    ).then_inc(max_done, 1)
                        k = i - 1
                        if 0 <= k < NU:
                            dve.wait_ge(exp_done, k + 1)
                            m = 8 + 4 * (k % 4)
                            link(nc.vector.reciprocal(small[:, m + 2:m + 4], small[:, m + 2:m + 4]))
                            if UNITS[k][7] is not None:
                                h = UNITS[k][4] - A_HEADS - B_HEADS
                                link(nc.vector.tensor_tensor(small[:, m + 2:m + 4], small[:, m + 2:m + 4],
                                                             gate[:, :, h, UNITS[k][7]], ALU.mult))
                            nc.vector.tensor_scalar(E[:, k % 3, 0:SEQ], E[:, k % 3, 0:SEQ], small[:, m + 3:m + 4],
                                                    None, ALU.mult)
                            nc.vector.tensor_scalar(E[:, k % 3, SEQ:], E[:, k % 3, SEQ:], small[:, m + 2:m + 3],
                                                    None, ALU.mult).then_inc(scaled, 1)
                        k = i - 2
                        if 0 <= k < NU and k % 2 == 1:
                            dve.wait_ge(t_ready, k + 1)
                            if k >= 2:
                                dve.wait_ge(o_ready, k - 1)
                            nc.vector.tensor_copy(PT[:, k % 2, :], bank[3 + k % 2][:, 0:3 * P]).then_inc(pt_v, 1)
                        k = i - 4
                        if 0 <= k < NU and UNITS[k][6]:
                            dve.wait_ge(o_hi, HEADS_DONE[k])
                            o = UNITS[k][4]
                            nc.vector.tensor_tensor(actT_lo[:, o, :], bank[5 + HEADS_DONE[k] % 2][:, 0:SEQ],
                                                    actT_hi[:, o, :].bitcast(F32), ALU.subtract).then_inc(o_lo, 1)

                    def y_evac(Y, b, banks, chunks_done):
                        dve.wait_ge(mm_done, chunks_done)
                        for t in range(NT):
                            last = nc.vector.tensor_copy(Y[:, t, bass.ds(b * N, N)], banks[t][:])
                        last.then_inc(y_ev, 1)

                    def residual(Y, gb, k, squared, loads):
                        dve.wait_ge(ysq_done, squared)
                        link(nc.vector.tensor_reduce(stat[:, 0:2], ss_part[:], AX.X, ALU.add))
                        inverse_root(k)
                        dve.wait_ge(gb_in, 16 * loads)
                        for t in range(NT):
                            link(nc.vector.scalar_tensor_tensor(out=Y[:, t, :], in0=Y[:, t, :],
                                                                scalar=stat[:, 6 + t:7 + t], in1=gb[:],
                                                                op0=ALU.mult, op1=ALU.mult))
                            nc.vector.tensor_tensor(X[:, t, :], X[:, t, :], Y[:, t, :], ALU.add).then_inc(x_new, 1)

                    for i in range(4 * CPB):
                        lo(i, N, OUT_0 - W1_CHUNKS + i + 1)
                        if i % CPB == 3 and i > CPB:
                            b = i // CPB - 1
                            y_evac(Y_mix, b, bank[2 * (b % 2):2 * (b % 2) + 2], OUT_0 + CPB * (b + 1))
                    y_evac(Y_mix, OUT_BLOCKS - 1, bank[2:4], FF_0)
                    residual(Y_mix, gb_mix, 2, OUT_BLOCKS, 1)

                    dve.wait_ge(x_new, NT)
                    norm_rows(3, 2 * NT)
                    norm_T(1, KC // 2)

                    def hidden(j):
                        dve.wait_ge(mm_done, 2 * CPB * j + FF_0)
                        dve.wait_ge(silu_done, j)
                        for t in range(NT):
                            last = nc.vector.tensor_tensor(hrow[:, t, :], hrow[:, t, :], bank[2 + t][:], ALU.mult)
                        last.then_inc(h_ready, 1)

                    def hidden_lo(j, at):
                        dve.wait_ge(ht_hi, j)
                        for c in range(2):
                            last = nc.vector.tensor_tensor(
                                hT_lo[:, bass.ds(at + 2 * c, 2), :].rearrange("p c t -> p (c t)"), bank[4 + c][:],
                                hT_hi[:, bass.ds(at + 2 * c, 2), :].rearrange("p c t -> p (c t)").bitcast(F32),
                                ALU.subtract)
                        last.then_inc(ht_lo, 1)

                    def turn(j, first):
                        for i in range(2 * CPB):
                            lo(i, N, 2 * CPB * j + (FF_0 - W1_CHUNKS + i + 1))
                            if i == 3 and not first:
                                hidden(j)
                            if i == CPB + 4 and not first:
                                hidden_lo(j, 4 * j - 4)

                    turn(0, True)
                    with dve.Fori(1, FF_BLOCKS) as j:
                        turn(j, False)
                    hidden(FF_BLOCKS)
                    hidden_lo(FF_BLOCKS, 4 * FF_BLOCKS - 4)

                    with dve.Fori(0, OUT_BLOCKS // 2) as it:
                        for i in range(2 * DN_CHUNKS):
                            lo(i, N, 2 * DN_CHUNKS * it + (DN_0 - W1_CHUNKS + i + 1))
                            if i == DN_CHUNKS + 3:
                                y_evac(Y_ffn, 2 * it, bank[0:2], 2 * DN_CHUNKS * it + (DN_0 + DN_CHUNKS))
                        y_evac(Y_ffn, 2 * it + 1, bank[2:4], 2 * DN_CHUNKS * it + (DN_0 + 2 * DN_CHUNKS))
                    residual(Y_ffn, gb_ffn, 4, 2 * OUT_BLOCKS, 2)

                @block.tensor
                def _(pe):
                    def mm3(i, banks, xh, xl, k, n, first, last, count):
                        pe.wait_ge(lo_done, count)
                        hi = chunk_view(w_hi, i % RING, n)
                        lo = chunk_view(w_lo, i % RING, n)
                        for c in range(2):
                            for t in range(NT):
                                o = banks[t][:, 0:n]
                                a, b = xh[:, k + c, t * P:(t + 1) * P], xl[:, k + c, t * P:(t + 1) * P]
                                nc.tensor.matmul(o, a, hi[:, c, :], start=first and c == 0, stop=False)
                                nc.tensor.matmul(o, a, lo[:, c, :], start=False, stop=False)
                                ins = nc.tensor.matmul(o, b, hi[:, c, :], start=False, stop=last and c == 1)
                        ins.then_inc(mm_done, 1)

                    def norm_T(base):
                        for b in range(KC // 2):
                            if b == 0:
                                pe.wait_ge(xn_ready, (NT if base == 0 else 2 * NT))
                            if base + b >= 4:
                                pe.wait_ge(nt_lo, base + b - 3)
                            for c in range(2):
                                for t in range(NT):
                                    k = 2 * b + c
                                    ins = nc.tensor.transpose(bank[4 + b % 4][:, (2 * c + t) * P:(2 * c + t + 1) * P],
                                                              xn[:, t, k * P:(k + 1) * P], ident)
                            ins.then_inc(nt_ready, 1)
                        pe.wait_ge(nt_lo, base + KC // 2)

                    norm_T(0)

                    for i in range(2 * CPB):
                        mm3(i, bank[2 * (i // CPB):2 * (i // CPB) + 2], actT_hi, actT_lo, 2 * (i % CPB), IN_N,
                            i % CPB == 0, i % CPB == CPB - 1, i + 1)
                    with pe.Fori(1, IN_BLOCKS // 2) as it:
                        for i in range(2 * CPB):
                            if i % CPB == 0:
                                pe.wait_ge(ev_a, 2 * it - 1 + i // CPB)
                                pe.wait_ge(ev_v, 2 * it - 1 + i // CPB)
                            mm3(i, bank[2 * (i // CPB):2 * (i // CPB) + 2], actT_hi, actT_lo, 2 * (i % CPB), IN_N,
                                i % CPB == 0, i % CPB == CPB - 1, 2 * CPB * it + i + 1)

                    pe.wait_ge(pe_in, 32)
                    pe.wait_ge(ev_a, IN_BLOCKS)
                    pe.wait_ge(ev_v, IN_BLOCKS)
                    nc.tensor.transpose(bank[0][:, 0:2 * CMP_BLOCK], pe_rows[:, :],
                                        ident[0:2 * CMP_BLOCK, 0:2 * CMP_BLOCK]).then_inc(pe_t, 1)
                    pe.wait_ge(roped, 1)
                    for k in range(PAIRS):
                        if k >= 4:
                            if k % 2 == 0:
                                pe.wait_ge(qt_a, (k - 4) // 2 + 1)
                            else:
                                pe.wait_ge(qt_v, (k - 4) // 2 + 1)
                        for c in range(2):
                            for t in range(NT):
                                ins = nc.tensor.transpose(bank[4 + k % 4][:, (2 * c + t) * P:(2 * c + t + 1) * P],
                                                          TILES[2 * k + c][0](t), ident)
                        ins.then_inc(qt_ready, 1)
                    pe.wait_ge(qt_a, PAIRS // 2 + 1)
                    pe.wait_ge(qt_v, PAIRS // 2)
                    pe.wait_ge(chain, 6)

                    for k, (t, heads) in enumerate(LOGITS):
                        if k >= 4:
                            pe.wait_ge(relu_done, k - 3)
                        width = SEQ if t else P
                        for n, h in enumerate(heads):
                            q = IDX_DIM * (h % 2)
                            ins = nc.tensor.matmul(bank[k % 4][:, n * width:(n + 1) * width],
                                                   QT[q:q + IDX_DIM, T_IQ + h // 2, t * P:(t + 1) * P],
                                                   QT[q:q + IDX_DIM, T_IK, 0:width], start=True, stop=True)
                        ins.then_inc(lg_ready, 1)

                    for i in range(W1_CHUNKS):
                        kv = i // 8
                        if i % 8 == 0:
                            pe.wait_ge(blk_done, kv + 1)
                        pe.wait_ge(raw_in[i % RING], 16 * ((W1_0 + i) // RING + 1))
                        w = raw[:, i % RING, :].rearrange("p (j h) -> p j h", j=4)
                        for jj in range(4):
                            j = (i % 8) * 4 + jj
                            for half in range(2):
                                ins = nc.tensor.matmul(bank[4 + 2 * kv + half][:, 0:GROUPS * N_CMP],
                                                       w[:, jj, half * P:(half + 1) * P],
                                                       blk[:, kv, j, :, :].rearrange("p g c -> p (g c)"),
                                                       start=(j == 0), stop=(j == CMP_BLOCK - 1))
                        ins.then_inc(mm_done, 1)
                    pe.wait_ge(w2_in, 32)
                    pe.wait_ge(gelu_done, 1)
                    for half in range(2):
                        nc.tensor.matmul(bank[4][:, 0:GROUPS * N_CMP], w2[:, 0, half, :], hid_k[:, half, :],
                                         start=(half == 0), stop=(half == 1))
                    pe.wait_ge(gelu_done, 2)
                    for g in range(GROUPS):
                        for half in range(2):
                            ins = nc.tensor.matmul(bank[4][:, P + g * HD:P + (g + 1) * HD],
                                                   hid_v[:, half, g].rearrange("p r c -> p (r c)"), w2[:, 1, half, :],
                                                   start=(half == 0), stop=(half == 1))
                    ins.then_inc(kv_ready, 1)
                    pe.wait_ge(kv_ev, 1)
                    for t in range(NT):
                        for h in range(C_HEADS):
                            g = h // 4
                            ins = nc.tensor.matmul(bank[5][:, (t * C_HEADS + h) * N_CMP:(t * C_HEADS + h + 1) * N_CMP],
                                                   QT[:, T_CQ + h, t * P:(t + 1) * P],
                                                   kcT[:, g * N_CMP:(g + 1) * N_CMP], start=True, stop=True)
                    ins.then_inc(csc_ready, 1)
                    pe.wait_ge(pc_ready, 1)
                    for g in range(GROUPS):
                        for t in range(NT):
                            ins = nc.tensor.transpose(bank[6][:, (g * NT + t) * P:(g * NT + t + 1) * P],
                                                      p_cmp[:, t, 4 * g:4 * g + 4, :].rearrange("p h c -> p (h c)"), ident)
                    ins.then_inc(pct_ready, 1)
                    pe.wait_ge(pct_ev, 1)
                    pe.wait_ge(relu_done, len(LOGITS))
                    pe.wait_ge(topk_done, 1)

                    for i in range(NU + 3):
                        if i < NU:
                            q, key, _, mask, *_ = UNITS[i]
                            if i >= 3:
                                pe.wait_ge(exp_done, i - 2)
                            o = bank[i % 3]
                            eye, m = {"dilated": (ident, dilated), "topk": (ident_b[:], topk_b[:]),
                                      "causal": (ident_b[:], causal_b[:])}[mask]
                            nc.tensor.matmul(o[:, 0:SEQ], QT[:, q, P:SEQ], QT[:, key, :], start=True, stop=False)
                            nc.tensor.matmul(o[:, 0:SEQ], eye, m[:, 0:SEQ], start=False, stop=True)
                            nc.tensor.matmul(o[:, SEQ:3 * P], QT[:, q, 0:P], QT[:, key, 0:P], start=True, stop=False)
                            nc.tensor.matmul(o[:, SEQ:3 * P], eye, m[:, SEQ:3 * P], start=False, stop=True
                                             ).then_inc(s_ready, 1)
                        k = i - 2
                        if 0 <= k < NU:
                            pe.wait_ge(scaled, k + 1)
                            if k >= 2:
                                if k % 2 == 0:
                                    pe.wait_ge(pt_a, k // 2)
                                else:
                                    pe.wait_ge(pt_v, k // 2)
                            o = bank[3 + k % 2]
                            nc.tensor.transpose(o[:, 0:P], E[:, k % 3, SEQ:3 * P], ident)
                            nc.tensor.transpose(o[:, P:2 * P], E[:, k % 3, 0:P], ident)
                            nc.tensor.transpose(o[:, 2 * P:3 * P], E[:, k % 3, P:2 * P], ident).then_inc(t_ready, 1)
                        k = i - 3
                        if 0 <= k < NU:
                            _, _, v, _, head, first, last, _ = UNITS[k]
                            if k % 2 == 0:
                                pe.wait_ge(pt_a, k // 2 + 1)
                            else:
                                pe.wait_ge(pt_v, k // 2 + 1)
                            n = HEADS_DONE[k] + (0 if last else 1)
                            o = bank[5 + n % 2]
                            if first and n >= 3:
                                pe.wait_ge(o_lo, n - 2)
                            begun = False
                            if first and head >= A_HEADS + B_HEADS:
                                h = head - A_HEADS - B_HEADS
                                r = 32 * (h % 4)
                                nc.tensor.matmul(o[:, 0:SEQ], vc[r:r + 32, h // 4, :], pcT[r:r + 32, h // 4, :],
                                                 start=True, stop=False)
                                begun = True
                            nc.tensor.matmul(o[:, 0:SEQ], rows[:, 0, v:v + HD], PT[:, k % 2, 0:SEQ],
                                             start=first and not begun, stop=False)
                            nc.tensor.matmul(o[:, P:SEQ], rows[:, 1, v:v + HD], PT[:, k % 2, SEQ:3 * P],
                                             start=False, stop=last).then_inc(o_ready, 1)
                    pe.wait_ge(o_lo, A_HEADS + B_HEADS + C_HEADS)

                    for i in range(4 * CPB):
                        b = i // CPB
                        if i % CPB == 0 and b >= 2:
                            pe.wait_ge(y_ev, b - 1)
                        mm3(i, bank[2 * (b % 2):2 * (b % 2) + 2], actT_hi, actT_lo, 2 * (i % CPB), N,
                            i % CPB == 0, i % CPB == CPB - 1, OUT_0 - W1_CHUNKS + i + 1)

                    norm_T(KC // 2)
                    pe.wait_ge(y_ev, OUT_BLOCKS)

                    def transpose_hidden(j):
                        pe.wait_ge(h_ready, j)
                        for c in range(4):
                            for t in range(NT):
                                ins = nc.tensor.transpose(
                                    bank[4 + c // 2][:, (2 * (c % 2) + t) * P:(2 * (c % 2) + t + 1) * P],
                                    hrow[:, t, c * P:(c + 1) * P], ident)
                        ins.then_inc(ht_ready, 1)

                    def turn(j, first):
                        for i in range(2 * CPB):
                            if i == 0 and not first:
                                pe.wait_ge(silu_done, j)
                            if i == CPB and not first:
                                transpose_hidden(j)
                            mm3(i, bank[2 * (i // CPB):2 * (i // CPB) + 2], actT_hi, actT_lo, 2 * (i % CPB), N,
                                i % CPB == 0, i % CPB == CPB - 1, 2 * CPB * j + (FF_0 - W1_CHUNKS + i + 1))
                        if not first:
                            pe.wait_ge(ht_lo, j)

                    turn(0, True)
                    with pe.Fori(1, FF_BLOCKS) as j:
                        turn(j, False)
                    transpose_hidden(FF_BLOCKS)
                    pe.wait_ge(ht_lo, FF_BLOCKS)

                    with pe.Fori(0, OUT_BLOCKS // 2) as it:
                        for i in range(2 * DN_CHUNKS):
                            b = i // DN_CHUNKS
                            if i % DN_CHUNKS == 0:
                                pe.wait_ge(y_ev, 2 * it + (OUT_BLOCKS - 1 + b))
                            mm3(i, bank[2 * b:2 * b + 2], hT_hi, hT_lo, 2 * (i % DN_CHUNKS), N,
                                i % DN_CHUNKS == 0, i % DN_CHUNKS == DN_CHUNKS - 1,
                                2 * DN_CHUNKS * it + (DN_0 - W1_CHUNKS + i + 1))

            nc.gpsimd.sem_clear(range(sems[0].num, sems[-1].num + 1))
            nc.all_engine_barrier()

        with nc.Block() as block:
            @block.sync
            def _(sp):
                sp.dma_start(out[0].rearrange("(t p) d -> p t d", p=P), X[:]).then_inc(x_out, 16)
                sp.wait_ge(x_out, 16)


_INS = ["x", "w_in", "w_out", "cmp_pe_k", "cmp_w1_k", "cmp_w2_k", "cmp_pe_v", "cmp_w1_v", "cmp_w2_v",
        "w_gate", "w_up", "w_down", "g_pre_mix", "g_post_mix", "g_pre_ffn", "g_post_ffn"]


def kernel(**inputs):
    import numpy as np
    import concourse.bacc as bacc
    from concourse.bass_utils import run_bass_kernel_spmd

    nc = bacc.Bacc("TRN2", target_bir_lowering=False, num_devices=1)
    arrays, args = {}, []
    for name in _INS:
        arrays[f"in_{name}"] = np.ascontiguousarray(inputs[name])
        args.append(nc.dram_tensor(f"in_{name}", arrays[f"in_{name}"].shape, F32, kind="ExternalInput").ap())
    arrays["consts"] = constants()
    args.append(nc.dram_tensor("consts", arrays["consts"].shape, F32, kind="ExternalInput").ap())
    args.append(nc.dram_tensor("out", (1, SEQ, D), F32, kind="ExternalOutput").ap())
    hybrid_trunk(nc, *args)
    r = run_bass_kernel_spmd(nc, [arrays], core_ids=[0])
    return r.results[0]["out"]
```

```python
from contextlib import ExitStack

import concourse.bass as bass
from concourse import mybir

F32 = mybir.dt.float32
F32R = mybir.dt.float32r
BF16 = mybir.dt.bfloat16
ACT = mybir.ActivationFunctionType
ALU = mybir.AluOpType
AX = mybir.AxisListType

P = 128
SEQ = 256
NT = SEQ // P
D = 2048
KC = D // P
DEPTH = 2
HD = 128
A_HEADS, B_HEADS, C_HEADS = 4, 4, 8
IDX_HEADS, IDX_DIM = 16, 64
TOPK = 64
D_FF = 5632
SCALE = HD ** -0.5
EPS = 1e-6
CMP_BLOCK, CMP_STRIDE, CMP_HIDDEN = 32, 16, 256
N_CMP = SEQ // CMP_STRIDE - 1
GROUPS = 2
NEG = -1.0e30
TAKEN = -3.0e38

A_Q = 0
A_K = A_Q + A_HEADS * HD
A_V = A_K + HD
I_Q = A_V + HD
I_K = I_Q + IDX_HEADS * IDX_DIM
I_W = I_K + IDX_DIM
B_Q = I_W + IDX_HEADS
B_K = B_Q + B_HEADS * HD
B_V = B_K + B_HEADS * HD
C_Q = B_V + B_HEADS * HD
C_KC = C_Q + C_HEADS * HD
C_VC = C_KC + GROUPS * HD
C_KS = C_VC + GROUPS * HD
C_VS = C_KS + GROUPS * HD
C_KW = C_VS + GROUPS * HD
C_VW = C_KW + GROUPS * HD
C_G = C_VW + GROUPS * HD
IN_W = C_G + 3 * C_HEADS

IN_BLOCKS = 14
IN_N = IN_W // IN_BLOCKS
N = 512
OUT_BLOCKS = D // N
FF_BLOCKS = D_FF // N
FF_KC = D_FF // P

RING = 4
AHEAD = 3
CPB = KC // 2
W1_CHUNKS = 16
HALF = IN_BLOCKS // 2
FRONT = HALF * CPB
IN_TURNS = HALF * CPB
OUT_TURNS = OUT_BLOCKS * CPB
TURNS = IN_TURNS + OUT_TURNS
FF_0 = FRONT + TURNS
DN_0 = FF_0 + FF_BLOCKS * 2 * CPB
DN_CHUNKS = FF_KC // 2

T_CQR, T_KS, T_KW, T_CQ, T_KC, T_VC = 0, 8, 10, 12, 20, 22
T_IQ, T_BK, T_AQ, T_AK, T_IK, T_BQ = 0, 8, 12, 16, 17, 18
T_SLOTS = 24

K_ID = 0
K_CAUSAL = K_ID + P
K_DIL = K_CAUSAL + 3 * P
K_CBIAS = K_DIL + 3 * P
K_CKEEP = K_CBIAS + NT * N_CMP
K_NONE = K_CKEEP + NT * N_CMP
K_COS = K_NONE + NT
K_SIN = K_COS + NT * 64
K_ICOS = K_SIN + NT * 64
K_ISIN = K_ICOS + NT * 32
K_END = K_ISIN + NT * 32


def constants():
    import numpy as np

    out = np.zeros((P, K_END), np.float32)
    out[:, K_ID:K_ID + P] = np.eye(P, dtype=np.float32)
    t = np.arange(SEQ)[:, None]
    s = np.arange(SEQ)[None, :]

    def slab(full):
        return np.concatenate([full[P:, :], full[:P, :P]], axis=1)

    out[:, K_CAUSAL:K_CAUSAL + 3 * P] = slab(np.where(s <= t, 0.0, NEG))
    count = sum(((t - s >= 0) & (t - s <= w) & ((t - s) % d == 0)).astype(np.int64)
                for w, d in ((128, 1), (512, 4), (2048, 16)))
    out[:, K_DIL:K_DIL + 3 * P] = slab(np.where(count > 0, np.log(np.maximum(count, 1)) / SCALE, NEG))
    ends = np.arange(N_CMP) * CMP_STRIDE + CMP_BLOCK - 1
    seen = ends[None, :] <= t
    for i in range(NT):
        rows = seen[i * P:(i + 1) * P]
        out[:, K_CBIAS + i * N_CMP:K_CBIAS + (i + 1) * N_CMP] = np.where(rows, 0.0, NEG)
        out[:, K_CKEEP + i * N_CMP:K_CKEEP + (i + 1) * N_CMP] = rows
        out[:, K_NONE + i] = ~rows.any(axis=1)
        for at_c, at_s, half in ((K_COS, K_SIN, 64), (K_ICOS, K_ISIN, 32)):
            dim = 2 * half
            inv = np.float32(1.0) / (np.float32(10000.0) ** (np.arange(0, dim, 2, dtype=np.float32) / np.float32(dim)))
            angle = np.arange(i * P, (i + 1) * P, dtype=np.float32)[:, None] * inv[None, :].astype(np.float32)
            out[:, at_c + i * half:at_c + (i + 1) * half] = np.cos(angle)
            out[:, at_s + i * half:at_s + (i + 1) * half] = np.sin(angle)
    return out


def hybrid_trunk(nc, x, w_in, w_out, pe_k, w1_k, w2_k, pe_v, w1_v, w2_v, w_gate, w_up, w_down,
                 g_pre_mix, g_post_mix, g_pre_ffn, g_post_ffn, consts, out):
    with ExitStack() as ctx:
        def sb(name, shape, dt=F32, where=ctx):
            return where.enter_context(nc.sbuf_tensor(name, shape, dt))

        X = sb("X", [P, NT, D])
        raw = sb("raw", [P, RING, 2 * N])
        KON = sb("KON", [P, K_END])
        ident_b = sb("ident_b", [P, P], BF16)
        causal_b = sb("causal_b", [P, 3 * P], BF16)
        topk_b = sb("topk_b", [P, 3 * P], BF16)
        gain_rows = sb("gain_rows", [4 * KC, P])
        gain_all = sb("gain_all", [P, 4 * KC])
        gain = sb("gain", [P, 2, KC])
        pe_rows = sb("pe_rows", [2 * CMP_BLOCK, P])
        pe_T = sb("pe_T", [P, 2, CMP_BLOCK])
        w2 = sb("w2", [P, 2, 2, HD])
        hid_v = sb("hid_v", [P, 2, GROUPS, 4, 32])
        p_cmp = sb("p_cmp", [P, NT, C_HEADS, 32])
        stat = sb("stat", [P, 48])
        ss_part = sb("ss_part", [P, NT, OUT_BLOCKS])

        with ExitStack() as s1:
            actT_hi = sb("actT_hi", [P, KC, SEQ], F32R, s1)
            actT_lo = sb("actT_lo", [P, KC, SEQ], F32R, s1)
        with ExitStack() as s1:
            Y_ffn = sb("Y_ffn", [P, NT, D], F32, s1)
            gb_ffn = sb("gb_ffn", [P, D], F32, s1)
            sq_ffn = sb("sq_ffn", [P, 2, NT, N], F32, s1)
        sb("place_act", [P, 2 * KC * SEQ])

        w_hi = sb("w_hi", [P, RING, 2 * N], F32R)
        w_lo = sb("w_lo", [P, RING, 2 * N], F32R)

        with ExitStack() as s1:
            with ExitStack() as s2:
                rows_r = sb("rows_r", [P, NT, IN_W], F32R, s2)
            rows = sb("rows", [P, NT, IN_W], F32, s1)
            with ExitStack() as s2:
                sq_x = sb("sq_x", [P, NT, D], F32, s2)
            with ExitStack() as s2:
                sq_mix = sb("sq_mix", [P, OUT_BLOCKS, NT, N], F32, s2)
            QT = sb("QT", [P, T_SLOTS, SEQ], F32, s1)
            with ExitStack() as s2:
                cqr = sb("cqr", [P, NT, C_HEADS * HD], F32, s2)
            with ExitStack() as s2:
                blk = sb("blk", [P, 2, CMP_BLOCK, GROUPS, N_CMP], F32, s2)
                hid_k = sb("hid_k", [P, 2, GROUPS * N_CMP], F32, s2)
            with ExitStack() as s2:
                relu = sb("relu", [P, 2, N], F32, s2)
                acc = sb("acc", [P, 3 * P], F32, s2)
                work = sb("work", [P, 3 * P], F32, s2)
            gb_mix = sb("gb_mix", [P, D], F32, s1)
            rt = sb("rt", [P, 4, 256], F32, s1)
            ik2 = sb("ik2", [P, NT, 2 * IDX_DIM], F32, s1)
            with ExitStack() as s2:
                w1 = sb("w1", [P, 2, 4, CMP_HIDDEN], F32, s2)
            E = sb("E", [P, 2, 3 * P], F32, s1)
            PT = sb("PT", [P, 2, 3 * P], F32, s1)
            kcT = sb("kcT", [P, GROUPS * N_CMP], F32, s1)
            vc = sb("vc", [P, GROUPS, HD], F32, s1)
            sc = sb("sc", [P, NT, C_HEADS, N_CMP], F32, s1)
            pcT = sb("pcT", [P, GROUPS, SEQ], F32, s1)
            gate = sb("gate", [P, NT, C_HEADS, 3], F32, s1)
            small = sb("small", [P, 96], F32, s1)
        with ExitStack() as s1:
            hT_hi = sb("hT_hi", [P, FF_KC, SEQ], F32R, s1)
            hT_lo = sb("hT_lo", [P, FF_KC, SEQ], F32R, s1)
            hrow = sb("hrow", [P, NT, N], F32, s1)
        Y_mix = rows[:, :, 0:D]
        kvT = QT[:, T_KC:T_KC + 4, :].rearrange("p (k g) t -> p k g t", g=GROUPS)

        bank = [ctx.enter_context(nc.psum_tensor(f"bank{i}", [P, N], F32)) for i in range(8)]
        ident = KON[:, K_ID:K_ID + P]
        causal = KON[:, K_CAUSAL:K_CAUSAL + 3 * P]
        dilated = KON[:, K_DIL:K_DIL + 3 * P]

        x_in = [ctx.enter_context(nc.semaphore(f"x_in{i}")) for i in range(4)]
        first_in = [ctx.enter_context(nc.semaphore(f"first_in{i}")) for i in range(RING)]
        sems = []

        def sem(name):
            sems.append(ctx.enter_context(nc.semaphore(name)))
            return sems[-1]

        loaded = sem("loaded")
        gains_T = sem("gains_T")
        raw_in = [sem(f"raw_in{i}") for i in range(RING)]
        hi_done = sem("hi_done")
        lo_done = sem("lo_done")
        mm_done = sem("mm_done")
        sq_done = sem("sq_done")
        ysq_done = sem("ysq_done")
        ms_ready = sem("ms_ready")
        sd_ready = sem("sd_ready")
        r_ready = sem("r_ready")
        nt_ready = sem("nt_ready")
        nt_hi = sem("nt_hi")
        nt_lo = sem("nt_lo")
        x_new = sem("x_new")
        gain_ready = sem("gain_ready")
        ev_a = sem("ev_a")
        ev_v = sem("ev_v")
        rot = sem("rot")
        pe_in = sem("pe_in")
        w2_in = sem("w2_in")
        gb_in = sem("gb_in")
        bank_ready = [sem(f"bank_ready{i}") for i in range(3)]
        bank_free = [sem(f"bank_free{i}") for i in range(3)]
        acc_done = sem("acc_done")
        topk_done = sem("topk_done")
        blk_done = sem("blk_done")
        w1_in = [sem(f"w1_in{i}") for i in range(4)]
        w1_done = sem("w1_done")
        gelu_done = sem("gelu_done")
        csub = sem("csub")
        cexp = sem("cexp")
        pc_ready = sem("pc_ready")
        gexp = sem("gexp")
        max_done = sem("max_done")
        scaled = sem("scaled")
        o_ready = sem("o_ready")
        o_hi = sem("o_hi")
        o_lo = sem("o_lo")
        y_ev = sem("y_ev")
        silu_done = sem("silu_done")
        h_ready = sem("h_ready")
        ht_ready = sem("ht_ready")
        ht_hi = sem("ht_hi")
        ht_lo = sem("ht_lo")
        chain = sem("chain")
        y_scaled = sem("y_scaled")
        x_out = sem("x_out")

        PIECES = [(C_Q, 4, HD), (C_Q + 512, 4, HD), (C_KS, 2, HD), (C_KW, 2, HD), (A_Q, 4, HD), (A_K, 1, HD),
                  (I_Q, 8, IDX_DIM), (I_Q + 512, 8, IDX_DIM), (I_K, 1, IDX_DIM), (B_Q, 4, HD), (B_K, 4, HD)]
        NONE, CQ0, CQ1, KS, KW, AQ, AK, IQ0, IQ1, IK, BQ, BK = range(12)

        def two(col):
            return [lambda t: rows[:, t, col:col + P], lambda t: rows[:, t, col + P:col + 2 * P]]

        PAIRS = [(i // 2, [lambda t, h=2 * i + c: cqr[:, t, h * HD:(h + 1) * HD] for c in range(2)],
                  T_CQR + 2 * i, CQ0 if i < 2 else CQ1) for i in range(4)]
        PAIRS += [(1, two(C_KC), T_KC, NONE), (2, two(C_VC), T_VC, NONE)]
        PAIRS += [(6, two(C_KS), T_KS, KS), (7, two(C_KW), T_KW, KW)]
        PAIRS += [(24 + i // 2, two(C_Q + 2 * i * P), T_CQ + 2 * i, NONE) for i in range(4)]
        LAST_CQ = len(PAIRS) - 1
        PAIRS += [(42 + i // 2, two(I_Q + 2 * i * P), T_IQ + 2 * i, IQ0 if i < 2 else IQ1) for i in range(4)]
        PAIRS += [(44, [lambda t: rows[:, t, A_K:A_K + P], lambda t: ik2[:, t, :]], T_AK, IK)]
        LAST_AI = len(PAIRS) - 1
        PAIRS += [(50 + i, two(A_Q + 2 * i * P), T_AQ + 2 * i, AQ) for i in range(2)]
        PAIRS += [(53 + i, two(B_Q + 2 * i * P), T_BQ + 2 * i, BQ) for i in range(2)]
        PAIRS += [(58 + i, two(B_K + 2 * i * P), T_BK + 2 * i, BK) for i in range(2)]
        LAST_B = len(PAIRS) - 1

        LOGITS = [(1, [4 * g + odd, 4 * g + 2 + odd]) for g in range(4) for odd in range(2)]
        LOGITS += [(0, [8 * g + 2 * j + odd for j in range(4)]) for g in range(2) for odd in range(2)]

        UNITS = []
        for h in range(C_HEADS):
            g = h // 4
            o = A_HEADS + B_HEADS + h
            UNITS += [(T_CQR + h, T_KS + g, C_VS + g * HD, "causal", o, True, False, 1),
                      (T_CQR + h, T_KW + g, C_VW + g * HD, "causal", o, False, True, 2)]
        UNITS += [(T_AQ + h, T_AK, A_V, "topk", h, True, True, None) for h in range(A_HEADS)]
        UNITS += [(T_BQ + h, T_BK + h, B_V + h * HD, "dilated", A_HEADS + h, True, True, None)
                  for h in range(B_HEADS)]
        NU = len(UNITS)
        HEADS_DONE = []
        done = 0
        for u in UNITS:
            done += u[6]
            HEADS_DONE.append(done)
        C_UNITS = 2 * C_HEADS

        W1_TURN = [4 + 5 * i // 4 for i in range(W1_CHUNKS)]
        GELU_TURN, KV_TURN, CSC_TURN, PCT_TURN, LOGIT_TURN = 24, 25, 26, 29, 45
        TOPK_TURNS = {turn: 1 for turn in range(48, 56)}
        SCORE_TURN = [CSC_TURN + u if u < C_UNITS else IN_TURNS + u - C_UNITS for u in range(NU)]
        Y_CUT = 896
        WORK = []
        for turn in range(TURNS):
            todo = [("T", u) for u in range(NU) if SCORE_TURN[u] + 2 == turn]
            todo += [("S", u) for u in range(NU) if SCORE_TURN[u] == turn]
            todo += [("pair", k) for k, pair in enumerate(PAIRS) if pair[0] == turn]
            todo += [("w1", i) for i in range(W1_CHUNKS) if W1_TURN[i] == turn]
            todo += [("logit", k) for k in range(len(LOGITS)) if LOGIT_TURN + k // 4 == turn]
            todo += [(name, 0) for name, at in (("pe", 0), ("kv", KV_TURN), ("csc", CSC_TURN), ("pct", PCT_TURN))
                     if at == turn]
            todo += [("PV", u) for u in range(NU) if SCORE_TURN[u] + 3 == turn]
            WORK.append(todo)
        USE = {}
        for todo in WORK:
            for what in todo:
                if what[0] not in ("w1", "PV"):
                    USE[what] = len(USE)

        def scratch(what):
            return bank[4 + USE[what] % 3]

        def filled(engine, what):
            engine.wait_ge(bank_ready[USE[what] % 3], USE[what] // 3 + 1)

        def emptied(engine, what):
            engine.wait_ge(bank_free[USE[what] % 3], USE[what] // 3 + 1)

        def w1_slot(i):
            at = T_CQ + 4 * (i % 4 - 2)
            return w1[:, i % 4] if i % 4 < 2 else QT[:, at:at + 4, :]

        O_BANK = bank[7]

        OUT_ORDER = [(b, k) for b in range(2) for k in range(4, 8)]
        OUT_ORDER += [(0, 0), (0, 1), (1, 0), (1, 1), (0, 2), (0, 3), (1, 2), (1, 3)]
        OUT_ORDER += [(b, k) for b in range(2, OUT_BLOCKS) for k in range(CPB)]
        Y_TURNS = {70: 0, 72: 1, 80: 2}
        C_HI = [C_Q + h * HD for h in range(C_HEADS)]
        C_LO = [C_KC + h * HD for h in range(4)] + [C_KS, C_KS + HD, C_KW, C_KW + HD]

        def o_place(head, part):
            h = head - A_HEADS - B_HEADS
            if h < 0:
                return (actT_hi, actT_lo)[part][:, head, :].rearrange("p (t s) -> p t s", t=NT)
            col = (C_HI, C_LO)[part][h]
            return rows_r[:, :, col:col + P]

        def chunk_view(buf, slot, n):
            return buf[:, slot, 0:2 * n].rearrange("p (c n) -> p c n", c=2)

        def load_first(sp, i, of_layer):
            src = w_in[bass.ds(of_layer, 1), i * 2 * P:(i + 1) * 2 * P, HALF * IN_N:(HALF + 1) * IN_N]
            sp.dma_start(chunk_view(raw, i, IN_N), src.rearrange("l (c p) n -> p (l c) n", p=P)
                         ).then_inc(first_in[i], 16)

        with nc.Block() as block:
            @block.sync
            def _(sp):
                sp.dma_start(KON[:], consts).then_inc(loaded, 16)
                for i, g in enumerate((g_pre_mix, g_pre_ffn)):
                    sp.dma_start(gain_rows[i * DEPTH * KC:(i + 1) * DEPTH * KC, :],
                                 g.rearrange("l (c p) -> (l c) p", p=P)).then_inc(loaded, 16)
                for i in range(4):
                    cols = slice(i * (D // 4), (i + 1) * (D // 4))
                    sp.dma_start(X[:, :, cols], x[0, :, cols].rearrange("(t p) d -> p t d", p=P)).then_inc(x_in[i], 16)
                    load_first(sp, i, 0)

            @block.gpsimd
            def _(pool):
                nc.gpsimd.memset(hid_v[:], 0.0)
                nc.gpsimd.memset(p_cmp[:], 0.0)

            @block.vector
            def _(dve):
                dve.wait_ge(loaded, 48)
                nc.vector.tensor_copy(ident_b[:], ident)
                nc.vector.tensor_copy(causal_b[:], causal)
                dve.wait_ge(gains_T, 1)
                nc.vector.tensor_copy(gain_all[:], bank[0][:, 0:4 * KC])

            @block.tensor
            def _(pe):
                pe.wait_ge(loaded, 48)
                nc.tensor.transpose(bank[0][:, 0:4 * KC], gain_rows[:, :],
                                    ident[0:4 * KC, 0:4 * KC]).then_inc(gains_T, 1)
        nc.gpsimd.sem_clear(range(sems[0].num, sems[-1].num + 1))
        nc.all_engine_barrier()

        with nc.Fori(0, DEPTH) as layer:
            with nc.Block() as block:

                @block.sync
                def _(sp):
                    def w_chunk(w, row, col, n):
                        return w[bass.ds(layer, 1), row:row + 2 * P, bass.ds(col, n)].rearrange(
                            "l (c p) n -> p (l c) n", p=P)

                    def load(i, src, n):
                        sp.dma_start(chunk_view(raw, i % RING, n), src).then_inc(raw_in[i % RING], 16)

                    for i in range(RING, 3 * CPB):
                        sp.wait_ge(lo_done, i - RING + 1)
                        load(i, w_chunk(w_in, (i % CPB) * 2 * P, (HALF + i // CPB) * IN_N, IN_N), IN_N)
                        if i == 2 * RING:
                            sp.dma_start(pe_rows[0:CMP_BLOCK, :], pe_k[bass.ds(layer, 1)].rearrange("l j d -> (l j) d")
                                         ).then_inc(pe_in, 16)
                            sp.dma_start(pe_rows[CMP_BLOCK:, :], pe_v[bass.ds(layer, 1)].rearrange("l j d -> (l j) d")
                                         ).then_inc(pe_in, 16)
                            for kv, w in enumerate((w2_k, w2_v)):
                                sp.dma_start(w2[:, kv], w[bass.ds(layer, 1)].rearrange(
                                    "l (h p) d -> p (l h) d", p=P)).then_inc(w2_in, 16)
                    with sp.Fori(1, 3) as it:
                        for i in range(2 * CPB):
                            sp.wait_ge(lo_done, 2 * CPB * it + (CPB + i - RING + 1))
                            load(i, w_chunk(w_in, (i % CPB) * 2 * P, (2 * it + (HALF + 1 + i // CPB)) * IN_N, IN_N),
                                 IN_N)

                    with sp.Fori(0, HALF) as b:
                        for i in range(CPB):
                            sp.wait_ge(lo_done, CPB * b + (FRONT + i - RING + 1))
                            load(i, w_chunk(w_in, i * 2 * P, b * IN_N, IN_N), IN_N)

                    for i, (b, k) in enumerate(OUT_ORDER):
                        sp.wait_ge(lo_done, FRONT + IN_TURNS + i - RING + 1)
                        load(i, w_chunk(w_out, k * 2 * P, b * N, N), N)
                        if i == CPB:
                            sp.wait_ge(topk_done, 1)
                            sp.dma_start(gb_mix[:], g_post_mix[bass.ds(layer, 1), :].partition_broadcast(P)
                                         ).then_inc(gb_in, 16)

                    with sp.Fori(0, FF_BLOCKS) as j:
                        for i in range(2 * CPB):
                            sp.wait_ge(lo_done, 2 * CPB * j + (FF_0 + i - RING + 1))
                            load(i, w_chunk(w_gate if i < CPB else w_up, (i % CPB) * 2 * P, j * N, N), N)

                    with sp.Fori(0, OUT_BLOCKS // 2) as it:
                        for i in range(2 * DN_CHUNKS):
                            sp.wait_ge(lo_done, 2 * DN_CHUNKS * it + (DN_0 + i - RING + 1))
                            load(i, w_chunk(w_down, (i % DN_CHUNKS) * 2 * P, (2 * it + i // DN_CHUNKS) * N, N), N)
                            if i == 2 * RING:
                                sp.wait_ge(mm_done, 2 * DN_CHUNKS * it + DN_0)
                                sp.dma_start(gb_ffn[:, bass.ds(it * 2 * N, 2 * N)],
                                             g_post_ffn[bass.ds(layer, 1), bass.ds(it * 2 * N, 2 * N)]
                                             .partition_broadcast(P)).then_inc(gb_in, 16)

                    for i in range(RING):
                        sp.wait_ge(lo_done, DN_0 + OUT_BLOCKS * DN_CHUNKS - RING + 1 + i)
                        load_first(sp, i, 1 - layer)

                @block.gpsimd
                def _(pool):
                    steps = 0
                    for k, (col, heads, width) in enumerate(PIECES):
                        half = width // 2
                        blocks = range(col // IN_N, (col + heads * width - 1) // IN_N + 1)
                        block_done = max((b - HALF) % IN_BLOCKS for b in blocks) + 1
                        pool.wait_ge(ev_a, block_done)
                        pool.wait_ge(ev_v, block_done)
                        at_c, at_s = (K_COS, K_SIN) if width == HD else (K_ICOS, K_ISIN)
                        for t in range(NT):
                            src = rows[:, t, col:col + heads * width].rearrange("p (h w) -> p h w", w=width)
                            x1, x2 = src[:, :, 0:half], src[:, :, half:width]
                            cos = KON[:, None, at_c + t * half:at_c + (t + 1) * half].to_broadcast([P, heads, half])
                            sin = KON[:, None, at_s + t * half:at_s + (t + 1) * half].to_broadcast([P, heads, half])
                            tmp = [rt[:, i, 0:heads * half].rearrange("p (h w) -> p h w", w=half) for i in range(4)]
                            if steps:
                                pool.wait_ge(rot, steps)
                            nc.gpsimd.tensor_tensor(tmp[0], x1, cos, ALU.mult)
                            nc.gpsimd.tensor_tensor(tmp[1], x2, sin, ALU.mult)
                            nc.gpsimd.tensor_tensor(tmp[2], x2, cos, ALU.mult)
                            nc.gpsimd.tensor_tensor(tmp[3], x1, sin, ALU.mult).then_inc(rot, 1)
                            steps += 1
                            pool.wait_ge(rot, steps)
                            if C_Q <= col < C_KC:
                                at = col - C_Q
                                dst = [cqr[:, t, at:at + heads * width].rearrange("p (h w) -> p h w", w=width)]
                            elif col == I_K:
                                dst = [ik2[:, t, c * width:(c + 1) * width].rearrange("p (h w) -> p h w", w=width)
                                       for c in range(2)]
                            else:
                                dst = [src]
                            for d in dst:
                                nc.gpsimd.tensor_tensor(d[:, :, 0:half], tmp[0], tmp[1], ALU.subtract)
                                last = nc.gpsimd.tensor_tensor(d[:, :, half:width], tmp[2], tmp[3], ALU.add)
                            last.then_inc(rot, 1)
                            steps += 1

                    pool.wait_ge(y_scaled, 1)
                    nc.gpsimd.tensor_tensor(X[:, 1, Y_CUT:], X[:, 1, Y_CUT:], Y_ffn[:, 1, Y_CUT:], ALU.add)

                @block.scalar
                def _(act):
                    def hi(i, n, loads, first=False):
                        if first:
                            act.wait_ge(first_in[i], 16 * layer + 16)
                        else:
                            act.wait_ge(raw_in[i % RING], loads)
                        nc.scalar.activation(w_hi[:, i % RING, 0:2 * n], raw[:, i % RING, 0:2 * n],
                                             ACT.Copy).then_inc(hi_done, 1)

                    def x_hi(which, base, b):
                        act.wait_ge(nt_ready, base + b + 1)
                        for c in range(2):
                            k = 2 * b + c
                            last = nc.scalar.activation(actT_hi[:, k, :], bank[4 + b % 4][:, c * SEQ:(c + 1) * SEQ],
                                                        ACT.Copy, scale=gain[:, which, k:k + 1])
                        last.then_inc(nt_hi, 1)

                    def squares(which, t):
                        if which == 0:
                            for i in range(4):
                                act.wait_ge(x_in[i], 16)
                        nc.scalar.activation(sq_x[:, t, :], X[:, t, :], ACT.Square,
                                             accum_out=stat[:, 10 * which + t:10 * which + t + 1]).then_inc(sq_done, 1)

                    def root(k, at):
                        act.wait_ge(ms_ready, k)
                        nc.scalar.activation(stat[:, at + 4:at + 6], stat[:, at + 2:at + 4], ACT.Sqrt
                                             ).then_inc(sd_ready, 1)

                    def in_evac(q, col, banks):
                        act.wait_ge(mm_done, CPB * (q + 1))
                        nc.scalar.activation(rows[:, 0, bass.ds(col, IN_N)], banks[0][:, 0:IN_N],
                                             ACT.Copy, scale=stat[:, 6:7]).then_inc(ev_a, 1)

                    act.wait_ge(gain_ready, 1)
                    for i in range(3 * CPB):
                        if i >= RING:
                            act.wait_ge(mm_done, i - RING + 1)
                        hi(i, IN_N, 16 * (i // RING), i < RING)
                        if i < CPB:
                            x_hi(0, 0, i)
                        if CPB - NT <= i < CPB:
                            squares(0, i - CPB + NT)
                        if i == CPB:
                            root(1, 0)
                        if i == CPB + 3:
                            act.wait_ge(r_ready, 1)
                            in_evac(0, HALF * IN_N, bank[0:2])
                        if i == 2 * CPB + 3:
                            in_evac(1, (HALF + 1) * IN_N, bank[2:4])
                    with act.Fori(1, 3) as it:
                        for i in range(2 * CPB):
                            act.wait_ge(mm_done, 2 * CPB * it + (CPB + i - RING + 1))
                            hi(i, IN_N, 16 * (2 * CPB // RING) * it + 16 * ((CPB + i) // RING))
                            if i == 3:
                                in_evac(2 * it, (2 * it + HALF) * IN_N, bank[0:2])
                            if i == CPB + 3:
                                in_evac(2 * it + 1, (2 * it + (HALF + 1)) * IN_N, bank[2:4])

                    def y_squares(sq, b, done, banks, chunks_done):
                        act.wait_ge(mm_done, chunks_done)
                        for t in range(NT):
                            if t == 1:
                                act.wait_ge(y_ev, 2 * done + 1)
                            nc.scalar.activation(sq[:, t, :], banks[t][:], ACT.Square,
                                                 accum_out=ss_part[:, t, bass.ds(b, 1)]).then_inc(ysq_done, 1)

                    def ff_hi(i, j):
                        act.wait_ge(mm_done, 2 * CPB * j + (FF_0 + i - RING + 1))
                        hi(i, N, 16 * (2 * CPB // RING) * j + 16 * ((FF_0 + i) // RING))

                    def gate_rows():
                        for t in range(NT):
                            last = nc.scalar.activation(hrow[:, t, :], bank[t][:], ACT.Silu,
                                                        scale=stat[:, 16 + t:17 + t])
                        last.then_inc(silu_done, 1)

                    def turn_hi(m):
                        act.wait_ge(mm_done, m - RING + 1)
                        hi(m, IN_N if m < FRONT + IN_TURNS else N, 16 * (m // RING))

                    def load_w1(i):
                        w = (w1_k, w1_v)[i // 8]
                        j = (i % 8) * 4
                        act.dma_start(w1_slot(i), w[bass.ds(layer, 1), j * HD:(j + 4) * HD, :].rearrange(
                            "l (j d) h -> d (l j) h", d=HD)).then_inc(w1_in[i % 4], 16)

                    def scratch_hi(what):
                        kind, i = what
                        filled(act, what)
                        src = scratch(what)
                        if kind == "pe":
                            last = nc.scalar.activation(pe_T[:].rearrange("p k j -> p (k j)"),
                                                        src[:, 0:2 * CMP_BLOCK], ACT.Copy)
                        elif kind == "pair":
                            slot = PAIRS[i][2]
                            last = nc.scalar.activation(QT[:, slot:slot + 2, :].rearrange("p c t -> p (c t)"), src[:],
                                                        ACT.Copy)
                        elif kind == "kv":
                            nc.scalar.activation(kcT[:], src[:, 0:GROUPS * N_CMP], ACT.Copy)
                            last = nc.scalar.activation(vc[:].rearrange("p g d -> p (g d)"),
                                                        src[:, P:P + GROUPS * HD], ACT.Copy)
                        elif kind == "pct":
                            last = nc.scalar.activation(pcT[:].rearrange("p g t -> p (g t)"), src[:], ACT.Copy)
                        last.then_inc(bank_free[USE[what] % 3], 1)

                    for i in range(AHEAD):
                        turn_hi(FRONT + i)
                    for turn in range(TURNS):
                        if turn % CPB == 0 and turn <= IN_TURNS:
                            q = HALF - 1 + turn // CPB
                            in_evac(q, (q + HALF) % IN_BLOCKS * IN_N, bank[2 * (q % 2):2 * (q % 2) + 2])
                        for i in range(W1_CHUNKS):
                            if turn == (i if i < 4 else W1_TURN[i - 4] + 1):
                                if i >= 4:
                                    act.wait_ge(w1_done, i - 3)
                                load_w1(i)
                        for what in WORK[turn - 1] if turn else []:
                            kind, i = what
                            if kind in ("pe", "pair", "kv", "pct"):
                                scratch_hi(what)
                            elif kind == "logit":
                                filled(act, what)
                                if i >= 2:
                                    act.wait_ge(acc_done, i - 1)
                                nc.scalar.activation(relu[:, i % 2, :], scratch(what)[:], ACT.Relu,
                                                     scale=IDX_DIM ** -0.5 * IDX_HEADS ** -0.5
                                                     ).then_inc(bank_free[USE[what] % 3], 1)
                            elif kind == "S":
                                act.wait_ge(max_done, i + 1)
                                if i >= 2:
                                    filled(act, ("T", i - 2))
                                m = 8 + 4 * (i % 4)
                                src = scratch(what)
                                nc.scalar.activation(E[:, i % 2, 0:SEQ], src[:, 0:SEQ], ACT.Exp, scale=SCALE,
                                                     bias=small[:, m + 1:m + 2], accum_out=small[:, m + 3:m + 4])
                                nc.scalar.activation(E[:, i % 2, SEQ:], src[:, SEQ:3 * P], ACT.Exp, scale=SCALE,
                                                     bias=small[:, m:m + 1], accum_out=small[:, m + 2:m + 3]
                                                     ).then_inc(bank_free[USE[what] % 3], 1)
                            elif kind == "T":
                                filled(act, what)
                                if i >= 2:
                                    act.wait_ge(o_ready, i - 1)
                                nc.scalar.activation(PT[:, i % 2, :], scratch(what)[:, 0:3 * P], ACT.Copy
                                                     ).then_inc(bank_free[USE[what] % 3], 1)
                            elif kind == "PV" and UNITS[i][6]:
                                act.wait_ge(o_ready, i + 1)
                                nc.scalar.activation(o_place(UNITS[i][4], 0),
                                                     O_BANK[:, 0:SEQ].rearrange("p (t s) -> p t s", t=NT),
                                                     ACT.Copy).then_inc(o_hi, 1)
                        if turn == 2:
                            act.wait_ge(ev_v, HALF)
                            act.wait_ge(ev_a, HALF)
                            nc.scalar.activation(gate[:].rearrange("p t h b -> p t (h b)"),
                                                 rows[:, :, C_G:C_G + 3 * C_HEADS], ACT.Exp, scale=-1.0
                                                 ).then_inc(gexp, 1)
                        if turn == GELU_TURN:
                            act.wait_ge(w1_done, W1_CHUNKS)
                            for half in range(2):
                                nc.scalar.activation(hid_k[:, half, :], O_BANK[:, half * 32:half * 32 + GROUPS * N_CMP],
                                                     ACT.Gelu_apprx_tanh)
                            for half in range(2):
                                for r in range(4):
                                    last = nc.scalar.activation(
                                        hid_v[:, half, :, r, 0:N_CMP],
                                        O_BANK[:, 64 + half * 32:64 + half * 32 + GROUPS * N_CMP].rearrange(
                                            "p (g c) -> p g c", g=GROUPS), ACT.Gelu_apprx_tanh)
                            last.then_inc(gelu_done, 1)
                        if turn == CSC_TURN + 2:
                            act.wait_ge(csub, 1)
                            nc.scalar.activation(sc[:], sc[:], ACT.Exp).then_inc(cexp, 1)
                        if turn in Y_TURNS:
                            b = Y_TURNS[turn]
                            y_squares(sq_mix[:, b], b, b, bank[2 * (b % 2):2 * (b % 2) + 2], FRONT + turn)
                        if FRONT + AHEAD + turn < FF_0:
                            turn_hi(FRONT + AHEAD + turn)
                        else:
                            ff_hi(FRONT + AHEAD + turn - FF_0, 0)

                    nc.scalar.activation(stat[:, 40:41], KON[:, K_ID:K_ID + 1], ACT.Sqrt)
                    y_squares(sq_mix[:, OUT_BLOCKS - 1], OUT_BLOCKS - 1, OUT_BLOCKS - 1, bank[2:4], FF_0)
                    root(2, 20)
                    for i in range(AHEAD, 2 * CPB):
                        if i < CPB + AHEAD:
                            x_hi(1, KC // 2, i - AHEAD)
                        ff_hi(i, 0)
                        if i in (CPB + 3, CPB + 4):
                            act.wait_ge(x_new, KC // 2)
                            squares(1, i - CPB - 3)
                        if i == CPB + 5:
                            root(3, 10)
                        if i == CPB + 6:
                            act.wait_ge(r_ready, 3)
                            gate_rows()

                    def turn(j):
                        for i in range(2 * CPB):
                            ff_hi(i, j)
                            if i == CPB + 3:
                                act.wait_ge(ht_ready, j)
                                for c in range(2):
                                    last = nc.scalar.activation(
                                        hT_hi[:, bass.ds(4 * j - 4 + 2 * c, 2), :].rearrange("p c t -> p (c t)"),
                                        bank[4 + c][:], ACT.Copy)
                                last.then_inc(ht_hi, 1)
                                gate_rows()

                    with act.Fori(1, FF_BLOCKS) as j:
                        turn(j)

                    for it in range(OUT_BLOCKS // 2):
                        for i in range(2 * DN_CHUNKS):
                            act.wait_ge(mm_done, 2 * DN_CHUNKS * it + (DN_0 + i - RING + 1))
                            hi(i, N, 16 * (2 * DN_CHUNKS // RING) * it + 16 * ((DN_0 + i) // RING))
                            if it == 0 and i == CPB:
                                act.wait_ge(ht_ready, FF_BLOCKS)
                                for c in range(2):
                                    at = 4 * FF_BLOCKS - 4 + 2 * c
                                    last = nc.scalar.activation(hT_hi[:, at:at + 2, :].rearrange("p c t -> p (c t)"),
                                                                bank[4 + c][:], ACT.Copy)
                                last.then_inc(ht_hi, 1)
                            b = 2 * it + i // DN_CHUNKS - 1
                            if i % DN_CHUNKS == 3 and b >= 0:
                                y_squares(sq_ffn[:, b % 2], b, OUT_BLOCKS + b, bank[2 * (b % 2):2 * (b % 2) + 2],
                                          DN_0 + DN_CHUNKS * (b + 1))
                    nc.scalar.activation(stat[:, 41:42], KON[:, K_ID:K_ID + 1], ACT.Sqrt)
                    b = OUT_BLOCKS - 1
                    y_squares(sq_ffn[:, b % 2], b, OUT_BLOCKS + b, bank[2:4], DN_0 + DN_CHUNKS * (b + 1))
                    root(4, 30)
                    act.wait_ge(r_ready, 4)
                    act.wait_ge(y_ev, 4 * OUT_BLOCKS)
                    nc.scalar.activation(Y_ffn[:, 1, Y_CUT:], Y_ffn[:, 1, Y_CUT:], ACT.Copy, scale=stat[:, 37:38]
                                         ).then_inc(y_scaled, 1)

                @block.vector
                def _(dve):
                    steps = [0]

                    def link(ins):
                        steps[0] += 1
                        ins.then_inc(chain, 1)
                        dve.wait_ge(chain, steps[0])

                    def lo(i, n, count):
                        dve.wait_ge(hi_done, count)
                        s = i % RING
                        nc.vector.tensor_tensor(w_lo[:, s, 0:2 * n], raw[:, s, 0:2 * n],
                                                w_hi[:, s, 0:2 * n].bitcast(F32), ALU.subtract).then_inc(lo_done, 1)

                    def mean_square(at):
                        nc.vector.tensor_scalar(stat[:, at + 2:at + 4], stat[:, at:at + 2], 1.0 / D, EPS,
                                                ALU.mult, ALU.add).then_inc(ms_ready, 1)

                    def inverse_root(k, at):
                        a, m, c = stat[:, at + 6:at + 8], stat[:, at + 2:at + 4], stat[:, at + 8:at + 10]
                        dve.wait_ge(sd_ready, k)
                        link(nc.vector.reciprocal(a, stat[:, at + 4:at + 6]))
                        link(nc.vector.tensor_tensor(c, a, a, ALU.mult))
                        link(nc.vector.tensor_tensor(c, c, m, ALU.mult))
                        link(nc.vector.tensor_scalar(c, c, -0.5, 1.5, ALU.mult, ALU.add))
                        nc.vector.tensor_tensor(a, a, c, ALU.mult).then_inc(r_ready, 1)
                        dve.wait_ge(r_ready, k)

                    def x_lo(which, base, b):
                        dve.wait_ge(nt_hi, base + b + 1)
                        for c in range(2):
                            k = 2 * b + c
                            last = nc.vector.scalar_tensor_tensor(
                                out=actT_lo[:, k, :], in0=bank[4 + b % 4][:, c * SEQ:(c + 1) * SEQ],
                                scalar=gain[:, which, k:k + 1], in1=actT_hi[:, k, :].bitcast(F32),
                                op0=ALU.mult, op1=ALU.subtract)
                        last.then_inc(nt_lo, 1)

                    nc.vector.tensor_copy(
                        gain[:], gain_all[:].rearrange("p (w l c) -> p w l c", w=2, l=DEPTH)[:, :, bass.ds(layer, 1), :]
                        .rearrange("p w l c -> p w (l c)")).then_inc(gain_ready, 1)
                    dve.wait_ge(gain_ready, 1)

                    def in_evac(q, col, banks):
                        dve.wait_ge(mm_done, CPB * (q + 1))
                        nc.vector.tensor_scalar(rows[:, 1, bass.ds(col, IN_N)], banks[1][:, 0:IN_N],
                                                stat[:, 7:8], None, ALU.mult).then_inc(ev_v, 1)

                    for i in range(3 * CPB):
                        lo(i, IN_N, i + 1)
                        if i < CPB:
                            x_lo(0, 0, i)
                        if i == CPB:
                            dve.wait_ge(sq_done, NT)
                            mean_square(0)
                            inverse_root(1, 0)
                        if i == CPB + 3:
                            in_evac(0, HALF * IN_N, bank[0:2])
                        if i == 2 * CPB + 3:
                            in_evac(1, (HALF + 1) * IN_N, bank[2:4])
                    with dve.Fori(1, 3) as it:
                        for i in range(2 * CPB):
                            lo(i, IN_N, 2 * CPB * it + (CPB + i + 1))
                            if i == 3:
                                in_evac(2 * it, (2 * it + HALF) * IN_N, bank[0:2])
                            if i == CPB + 3:
                                in_evac(2 * it + 1, (2 * it + (HALF + 1)) * IN_N, bank[2:4])

                    def blocks(kv):
                        for g in range(GROUPS):
                            for h in range(2):
                                last = nc.vector.tensor_tensor(
                                    blk[:, kv, h * CMP_STRIDE:(h + 1) * CMP_STRIDE, g, :],
                                    kvT[:, kv, g, h * CMP_STRIDE:h * CMP_STRIDE + N_CMP * CMP_STRIDE].rearrange(
                                        "p (c j) -> p j c", j=CMP_STRIDE),
                                    pe_T[:, kv, h * CMP_STRIDE:(h + 1) * CMP_STRIDE].unsqueeze(2).to_broadcast(
                                        [P, CMP_STRIDE, N_CMP]), ALU.add)
                        last.then_inc(blk_done, 1)

                    def add_logits(k):
                        t, heads = LOGITS[k]
                        emptied(dve, ("logit", k))
                        cols = slice(0, SEQ) if t else slice(SEQ, 3 * P)
                        width = SEQ if t else P
                        begun = any(LOGITS[before][0] == t for before in range(k))
                        for n, h in enumerate(heads):
                            ins = nc.vector.scalar_tensor_tensor(
                                out=acc[:, cols], in0=relu[:, k % 2, n * width:(n + 1) * width],
                                scalar=rows[:, t, I_W + h:I_W + h + 1],
                                in1=acc[:, cols] if begun or n else causal[:, cols], op0=ALU.mult, op1=ALU.add)
                            if n < len(heads) - 1:
                                link(ins)
                        ins.then_inc(acc_done, 1)
                        dve.wait_ge(acc_done, k + 1)

                    def topk(r):
                        src = work if r else acc
                        nc.vector.max(small[:, 32:40], src[:, 0:SEQ])
                        link(nc.vector.max(small[:, 40:48], src[:, SEQ:]))
                        nc.vector.match_replace(work[:, 0:SEQ], small[:, 32:40], src[:, 0:SEQ], TAKEN)
                        link(nc.vector.match_replace(work[:, SEQ:], small[:, 40:48], src[:, SEQ:], TAKEN))

                    sc2 = sc[:].rearrange("p t h c -> p (t h) c")

                    def compressed_scores():
                        what = ("csc", 0)
                        filled(dve, what)
                        for t in range(NT):
                            ins = nc.vector.scalar_tensor_tensor(
                                out=sc[:, t], in0=scratch(what)[:, t * 120:(t + 1) * 120].rearrange(
                                    "p (h c) -> p h c", c=N_CMP), scalar=SCALE,
                                in1=KON[:, None, K_CBIAS + t * N_CMP:K_CBIAS + (t + 1) * N_CMP].to_broadcast(
                                    [P, C_HEADS, N_CMP]), op0=ALU.mult, op1=ALU.add)
                        ins.then_inc(bank_free[USE[what] % 3], 1)
                        emptied(dve, what)
                        link(nc.vector.tensor_reduce(small[:, 48:64], sc2, AX.X, ALU.max))
                        nc.vector.tensor_tensor(sc2, sc2, small[:, 48:64].unsqueeze(2).to_broadcast([P, 16, N_CMP]),
                                                ALU.subtract).then_inc(csub, 1)

                    def compressed_weights():
                        dve.wait_ge(cexp, 1)
                        for t in range(NT):
                            ins = nc.vector.tensor_tensor(
                                sc[:, t], sc[:, t], KON[:, None, K_CKEEP + t * N_CMP:K_CKEEP + (t + 1) * N_CMP]
                                .to_broadcast([P, C_HEADS, N_CMP]), ALU.mult)
                        link(ins)
                        link(nc.vector.tensor_reduce(small[:, 64:80], sc2, AX.X, ALU.add))
                        for t in range(NT):
                            ins = nc.vector.tensor_scalar(small[:, 64 + 8 * t:72 + 8 * t],
                                                          small[:, 64 + 8 * t:72 + 8 * t],
                                                          KON[:, K_NONE + t:K_NONE + t + 1], None, ALU.add)
                        link(ins)
                        link(nc.vector.reciprocal(small[:, 64:80], small[:, 64:80]))
                        link(nc.vector.tensor_tensor(small[:, 64:80], small[:, 64:80],
                                                     gate[:, :, :, 0].rearrange("p t h -> p (t h)"), ALU.mult))
                        nc.vector.tensor_tensor(p_cmp[:, :, :, 0:N_CMP].rearrange("p t h c -> p (t h) c"), sc2,
                                                small[:, 64:80].unsqueeze(2).to_broadcast([P, 16, N_CMP]), ALU.mult
                                                ).then_inc(pc_ready, 1)

                    def row_max(i):
                        what = ("S", i)
                        filled(dve, what)
                        m = 8 + 4 * (i % 4)
                        src = scratch(what)
                        nc.vector.tensor_reduce(small[:, m + 1:m + 2], src[:, 0:SEQ], AX.X, ALU.max, negate=True)
                        link(nc.vector.tensor_reduce(small[:, m:m + 1], src[:, SEQ:3 * P], AX.X, ALU.max, negate=True))
                        nc.vector.tensor_scalar(small[:, m:m + 2], small[:, m:m + 2], SCALE, None, ALU.mult
                                                ).then_inc(max_done, 1)

                    def scale_rows(i):
                        emptied(dve, ("S", i))
                        m = 8 + 4 * (i % 4)
                        link(nc.vector.reciprocal(small[:, m + 2:m + 4], small[:, m + 2:m + 4]))
                        if UNITS[i][7] is not None:
                            h = UNITS[i][4] - A_HEADS - B_HEADS
                            link(nc.vector.tensor_tensor(small[:, m + 2:m + 4], small[:, m + 2:m + 4],
                                                         gate[:, :, h, UNITS[i][7]], ALU.mult))
                        nc.vector.tensor_scalar(E[:, i % 2, 0:SEQ], E[:, i % 2, 0:SEQ], small[:, m + 3:m + 4],
                                                None, ALU.mult)
                        nc.vector.tensor_scalar(E[:, i % 2, SEQ:], E[:, i % 2, SEQ:], small[:, m + 2:m + 3],
                                                None, ALU.mult).then_inc(scaled, 1)

                    def y_evac(Y, gb, loads, b, done, banks, chunks_done):
                        dve.wait_ge(mm_done, chunks_done)
                        dve.wait_ge(gb_in, loads)
                        for t in (1, 0):
                            if t == 0:
                                dve.wait_ge(ysq_done, 2 * done + 1)
                            nc.vector.tensor_tensor(Y[:, t, bass.ds(b * N, N)], banks[t][:],
                                                    gb[:, bass.ds(b * N, N)], ALU.mult).then_inc(y_ev, 1)

                    def row_scale(k, at, squared):
                        dve.wait_ge(ysq_done, squared)
                        link(nc.vector.tensor_reduce(stat[:, at:at + 2], ss_part[:], AX.X, ALU.add))
                        mean_square(at)
                        inverse_root(k, at)

                    def residual(Y, at, b):
                        cols = slice(2 * b * P, 2 * (b + 1) * P)
                        for t in range(NT):
                            last = nc.vector.scalar_tensor_tensor(
                                out=X[:, t, cols], in0=Y[:, t, cols], scalar=stat[:, at + 6 + t:at + 7 + t],
                                in1=X[:, t, cols], op0=ALU.mult, op1=ALU.add)
                        last.then_inc(x_new, 1)

                    def hidden(j):
                        dve.wait_ge(mm_done, 2 * CPB * j + FF_0)
                        dve.wait_ge(silu_done, j)
                        for t in range(NT):
                            last = nc.vector.scalar_tensor_tensor(
                                out=hrow[:, t, :], in0=bank[2 + t][:], scalar=stat[:, 16 + t:17 + t],
                                in1=hrow[:, t, :], op0=ALU.mult, op1=ALU.mult)
                        last.then_inc(h_ready, 1)

                    def hidden_lo(j, at):
                        dve.wait_ge(ht_hi, j)
                        for c in range(2):
                            last = nc.vector.tensor_tensor(
                                hT_lo[:, bass.ds(at + 2 * c, 2), :].rearrange("p c t -> p (c t)"), bank[4 + c][:],
                                hT_hi[:, bass.ds(at + 2 * c, 2), :].rearrange("p c t -> p (c t)").bitcast(F32),
                                ALU.subtract)
                        last.then_inc(ht_lo, 1)

                    def ff_lo(i, j):
                        lo(i, N, 2 * CPB * j + (FF_0 + i + 1))

                    def turn_lo(m):
                        lo(m, IN_N if m < FRONT + IN_TURNS else N, m + 1)

                    for i in range(AHEAD - 1):
                        turn_lo(FRONT + i)
                    for turn in range(TURNS):
                        before = WORK[turn - 1] if turn else []
                        if turn % CPB == 0 and turn <= IN_TURNS:
                            q = HALF - 1 + turn // CPB
                            in_evac(q, (q + HALF) % IN_BLOCKS * IN_N, bank[2 * (q % 2):2 * (q % 2) + 2])
                        for kind, i in before:
                            if kind == "S":
                                row_max(i)
                        turn_lo(FRONT + AHEAD - 1 + turn)
                        for kind, i in before:
                            if kind == "PV" and UNITS[i][6]:
                                dve.wait_ge(o_hi, HEADS_DONE[i])
                                nc.vector.tensor_tensor(
                                    o_place(UNITS[i][4], 1), O_BANK[:, 0:SEQ].rearrange("p (t s) -> p t s", t=NT),
                                    o_place(UNITS[i][4], 0).bitcast(F32), ALU.subtract).then_inc(o_lo, 1)
                            if kind == "logit":
                                if i == 0:
                                    dve.wait_ge(ev_a, (I_W // IN_N - HALF) % IN_BLOCKS + 1)
                                add_logits(i)
                        for kind, i in before:
                            if kind == "S":
                                scale_rows(i)
                            if kind == "csc":
                                compressed_scores()
                        if turn == 4:
                            dve.wait_ge(gexp, 1)
                            link(nc.vector.tensor_scalar(gate[:], gate[:], 1.0, None, ALU.add))
                            link(nc.vector.reciprocal(gate[:], gate[:]))
                        if turn in (3, 4):
                            emptied(dve, ("pair", turn + 1))
                            blocks(turn - 3)
                        if turn == CSC_TURN + 2:
                            compressed_weights()
                        if turn in TOPK_TURNS:
                            r = sum(n for at, n in TOPK_TURNS.items() if at < turn)
                            for k in range(TOPK_TURNS[turn]):
                                topk(r + k)
                            if r + TOPK_TURNS[turn] == TOPK // 8:
                                link(nc.vector.tensor_scalar(work[:], work[:], TAKEN, -1.0, ALU.is_equal, ALU.add))
                                nc.vector.scalar_tensor_tensor(out=topk_b[:], in0=work[:], scalar=-NEG, in1=causal,
                                                               op0=ALU.mult, op1=ALU.add).then_inc(topk_done, 1)
                        if turn in Y_TURNS:
                            b = Y_TURNS[turn]
                            y_evac(Y_mix, gb_mix, 16, b, b, bank[2 * (b % 2):2 * (b % 2) + 2], FRONT + turn)

                    ff_lo(AHEAD - 1, 0)
                    y_evac(Y_mix, gb_mix, 16, OUT_BLOCKS - 1, OUT_BLOCKS - 1, bank[2:4], FF_0)
                    dve.wait_ge(y_ev, 2 * OUT_BLOCKS)
                    row_scale(2, 20, 2 * OUT_BLOCKS)
                    for b in range(AHEAD):
                        residual(Y_mix, 20, b)
                    for i in range(AHEAD, 2 * CPB):
                        if i < CPB + AHEAD:
                            x_lo(1, KC // 2, i - AHEAD)
                        if i < CPB:
                            residual(Y_mix, 20, i)
                        ff_lo(i, 0)
                        if i == CPB + 5:
                            dve.wait_ge(sq_done, 2 * NT)
                            mean_square(10)
                            inverse_root(3, 10)

                    with dve.Fori(1, FF_BLOCKS) as j:
                        for i in range(2 * CPB):
                            ff_lo(i, j)
                            if i == 3:
                                hidden(j)
                            if i == CPB + 4:
                                hidden_lo(j, 4 * j - 4)

                    for it in range(OUT_BLOCKS // 2):
                        for i in range(2 * DN_CHUNKS):
                            lo(i, N, 2 * DN_CHUNKS * it + (DN_0 + i + 1))
                            if it == 0 and i == 3:
                                hidden(FF_BLOCKS)
                            if it == 0 and i == CPB + 1:
                                hidden_lo(FF_BLOCKS, 4 * FF_BLOCKS - 4)
                            b = 2 * it + i // DN_CHUNKS - 1
                            if i % DN_CHUNKS == 3 and b >= 0:
                                y_evac(Y_ffn, gb_ffn, 16 * (b // 2) + 32, b, OUT_BLOCKS + b,
                                       bank[2 * (b % 2):2 * (b % 2) + 2], DN_0 + DN_CHUNKS * (b + 1))
                    b = OUT_BLOCKS - 1
                    y_evac(Y_ffn, gb_ffn, 16 * (b // 2) + 32, b, OUT_BLOCKS + b, bank[2:4], DN_0 + DN_CHUNKS * (b + 1))
                    dve.wait_ge(y_ev, 4 * OUT_BLOCKS)
                    row_scale(4, 30, 4 * OUT_BLOCKS)
                    for t, end in ((0, D), (1, Y_CUT)):
                        nc.vector.scalar_tensor_tensor(out=X[:, t, 0:end], in0=Y_ffn[:, t, 0:end],
                                                       scalar=stat[:, 36 + t:37 + t], in1=X[:, t, 0:end],
                                                       op0=ALU.mult, op1=ALU.add)

                @block.tensor
                def _(pe):
                    def mm3(i, banks, lhs, k, n, first, last, count):
                        pe.wait_ge(lo_done, count)
                        hi = chunk_view(w_hi, i % RING, n)
                        lo = chunk_view(w_lo, i % RING, n)
                        for c in range(2):
                            for t in range(NT):
                                o = banks[t][:, 0:n]
                                a, b = lhs(k + c, t)
                                nc.tensor.matmul(o, a, hi[:, c, :], start=first and c == 0, stop=False)
                                nc.tensor.matmul(o, a, lo[:, c, :], start=False, stop=False)
                                ins = nc.tensor.matmul(o, b, hi[:, c, :], start=False, stop=last and c == 1)
                        ins.then_inc(mm_done, 1)

                    def x_lhs(k, t):
                        return actT_hi[:, k, t * P:(t + 1) * P], actT_lo[:, k, t * P:(t + 1) * P]

                    def o_lhs(k, t):
                        return o_place(k, 0)[:, t, :], o_place(k, 1)[:, t, :]

                    def h_lhs(k, t):
                        return hT_hi[:, k, t * P:(t + 1) * P], hT_lo[:, k, t * P:(t + 1) * P]

                    def x_T(base, b):
                        if base:
                            pe.wait_ge(x_new, b + 1)
                        else:
                            pe.wait_ge(x_in[b // 2], 16)
                        if base + b >= 4:
                            pe.wait_ge(nt_lo, base + b - 3)
                        for c in range(2):
                            for t in range(NT):
                                k = 2 * b + c
                                ins = nc.tensor.transpose(bank[4 + b % 4][:, (2 * c + t) * P:(2 * c + t + 1) * P],
                                                          X[:, t, k * P:(k + 1) * P], ident)
                        ins.then_inc(nt_ready, 1)

                    for b in range(AHEAD):
                        x_T(0, b)
                    for i in range(3 * CPB):
                        if i < CPB:
                            pe.wait_ge(nt_lo, i + 1)
                        q = i // CPB
                        if i == 2 * CPB:
                            pe.wait_ge(ev_a, 1)
                            pe.wait_ge(ev_v, 1)
                        mm3(i, bank[2 * (q % 2):2 * (q % 2) + 2], x_lhs, 2 * (i % CPB), IN_N,
                            i % CPB == 0, i % CPB == CPB - 1, i + 1)
                        if i + AHEAD < CPB:
                            x_T(0, i + AHEAD)
                    with pe.Fori(1, 3) as it:
                        for i in range(2 * CPB):
                            if i % CPB == 0:
                                pe.wait_ge(ev_a, 2 * it + i // CPB)
                                pe.wait_ge(ev_v, 2 * it + i // CPB)
                            q = 1 + i // CPB
                            mm3(i, bank[2 * (q % 2):2 * (q % 2) + 2], x_lhs, 2 * (i % CPB), IN_N,
                                i % CPB == 0, i % CPB == CPB - 1, 2 * CPB * it + (CPB + i + 1))

                    def vacant(what):
                        if USE[what] >= 3:
                            pe.wait_ge(bank_free[USE[what] % 3], USE[what] // 3)
                        return scratch(what)

                    def transpose_pair(k, o):
                        _, tiles, _, pieces = PAIRS[k]
                        if pieces:
                            pe.wait_ge(rot, 4 * pieces)
                        for c in range(2):
                            for t in range(NT):
                                ins = nc.tensor.transpose(o[:, (2 * c + t) * P:(2 * c + t + 1) * P],
                                                          tiles[c](t), ident)
                        return ins

                    def logits(k, o):
                        t, heads = LOGITS[k]
                        if k == 0:
                            emptied(pe, ("pair", LAST_AI))
                        width = SEQ if t else P
                        for n, h in enumerate(heads):
                            q = IDX_DIM * (h % 2)
                            ins = nc.tensor.matmul(o[:, n * width:(n + 1) * width],
                                                   QT[q:q + IDX_DIM, T_IQ + h // 2, t * P:(t + 1) * P],
                                                   QT[q:q + IDX_DIM, T_IK, 0:width], start=True, stop=True)
                        return ins

                    def hidden_rows(i):
                        kv = i // 8
                        pe.wait_ge(blk_done, kv + 1)
                        pe.wait_ge(w1_in[i % 4], 16 * (i // 4 + 1))
                        w = w1_slot(i)
                        for jj in range(4):
                            j = (i % 8) * 4 + jj
                            for half in range(2):
                                at = 64 * kv + 32 * half
                                ins = nc.tensor.matmul(O_BANK[:, at:at + GROUPS * N_CMP],
                                                       w[:, jj, half * P:(half + 1) * P],
                                                       blk[:, kv, j, :, :].rearrange("p g c -> p (g c)"),
                                                       start=(kv == 0 and j == 0 and half == 0),
                                                       stop=(kv == 1 and j == CMP_BLOCK - 1 and half == 1),
                                                       skip_group_check=True)
                        ins.then_inc(w1_done, 1)

                    def compressed_kv(o):
                        pe.wait_ge(w2_in, 32)
                        pe.wait_ge(gelu_done, 1)
                        for half in range(2):
                            nc.tensor.matmul(o[:, 0:GROUPS * N_CMP], w2[:, 0, half, :], hid_k[:, half, :],
                                             start=(half == 0), stop=(half == 1))
                        for g in range(GROUPS):
                            for half in range(2):
                                ins = nc.tensor.matmul(o[:, P + g * HD:P + (g + 1) * HD],
                                                       hid_v[:, half, g].rearrange("p r c -> p (r c)"),
                                                       w2[:, 1, half, :], start=(half == 0), stop=(half == 1))
                        return ins

                    def compressed_scores(o):
                        emptied(pe, ("kv", 0))
                        emptied(pe, ("pair", LAST_CQ))
                        for t in range(NT):
                            for h in range(C_HEADS):
                                g = h // 4
                                ins = nc.tensor.matmul(o[:, (t * C_HEADS + h) * N_CMP:(t * C_HEADS + h + 1) * N_CMP],
                                                       QT[:, T_CQ + h, t * P:(t + 1) * P],
                                                       kcT[:, g * N_CMP:(g + 1) * N_CMP], start=True, stop=True)
                        return ins

                    def compressed_weights(o):
                        pe.wait_ge(pc_ready, 1)
                        for g in range(GROUPS):
                            for t in range(NT):
                                ins = nc.tensor.transpose(
                                    o[:, (g * NT + t) * P:(g * NT + t + 1) * P],
                                    p_cmp[:, t, 4 * g:4 * g + 4, :].rearrange("p h c -> p (h c)"), ident)
                        return ins

                    def scores(u, o):
                        q, key, _, mask, *_ = UNITS[u]
                        if u == 0:
                            emptied(pe, ("pair", LAST_CQ))
                        if u == C_UNITS:
                            pe.wait_ge(topk_done, 1)
                        if u == C_UNITS + A_HEADS:
                            emptied(pe, ("pair", LAST_B))
                        eye, m = {"dilated": (ident, dilated), "topk": (ident_b[:], topk_b[:]),
                                  "causal": (ident_b[:], causal_b[:])}[mask]
                        nc.tensor.matmul(o[:, 0:SEQ], QT[:, q, P:SEQ], QT[:, key, :], start=True, stop=False)
                        nc.tensor.matmul(o[:, 0:SEQ], eye, m[:, 0:SEQ], start=False, stop=True)
                        nc.tensor.matmul(o[:, SEQ:3 * P], QT[:, q, 0:P], QT[:, key, 0:P], start=True, stop=False)
                        return nc.tensor.matmul(o[:, SEQ:3 * P], eye, m[:, SEQ:3 * P], start=False, stop=True)

                    def transposed_weights(u, o):
                        pe.wait_ge(scaled, u + 1)
                        nc.tensor.transpose(o[:, 0:P], E[:, u % 2, SEQ:3 * P], ident)
                        nc.tensor.transpose(o[:, P:2 * P], E[:, u % 2, 0:P], ident)
                        return nc.tensor.transpose(o[:, 2 * P:3 * P], E[:, u % 2, P:2 * P], ident)

                    def weighted_values(u):
                        _, _, v, _, head, first, last, _ = UNITS[u]
                        emptied(pe, ("T", u))
                        if first and HEADS_DONE[u] + (0 if last else 1) > 1:
                            pe.wait_ge(o_lo, HEADS_DONE[u] - (1 if last else 0))
                        o = O_BANK
                        compressed = last and head >= A_HEADS + B_HEADS
                        nc.tensor.matmul(o[:, 0:SEQ], rows[:, 0, v:v + HD], PT[:, u % 2, 0:SEQ],
                                         start=first, stop=False)
                        ins = nc.tensor.matmul(o[:, P:SEQ], rows[:, 1, v:v + HD], PT[:, u % 2, SEQ:3 * P],
                                               start=False, stop=last and not compressed)
                        if compressed:
                            emptied(pe, ("pct", 0))
                            h = head - A_HEADS - B_HEADS
                            r = 32 * (h % 4)
                            ins = nc.tensor.matmul(o[:, 0:SEQ], vc[r:r + 32, h // 4, :], pcT[r:r + 32, h // 4, :],
                                                   start=False, stop=True)
                        ins.then_inc(o_ready, 1)

                    for turn in range(TURNS):
                        if turn % CPB == 0 and turn < IN_TURNS:
                            pe.wait_ge(ev_a, HALF + turn // CPB - 1)
                            pe.wait_ge(ev_v, HALF + turn // CPB - 1)
                        if turn < IN_TURNS:
                            q = HALF + turn // CPB
                            mm3(turn, bank[2 * (q % 2):2 * (q % 2) + 2], x_lhs, 2 * (turn % CPB), IN_N,
                                turn % CPB == 0, turn % CPB == CPB - 1, FRONT + turn + 1)
                        else:
                            i = turn - IN_TURNS
                            b, k = OUT_ORDER[i]
                            if i in (0, 4):
                                pe.wait_ge(ev_a, IN_BLOCKS - (i == 0))
                                pe.wait_ge(ev_v, IN_BLOCKS - (i == 0))
                            if i in (2 * CPB, 3 * CPB):
                                pe.wait_ge(y_ev, 2 * (b - 1))
                                pe.wait_ge(ysq_done, 2 * (b - 1))
                            if OUT_ORDER[i] in ((0, 4), (0, 0), (0, 2)):
                                pe.wait_ge(o_lo, {4: 8, 0: 12, 2: 16}[k])
                            mm3(turn, bank[2 * (b % 2):2 * (b % 2) + 2], o_lhs, 2 * k, N,
                                b not in [x[0] for x in OUT_ORDER[:i]], b not in [x[0] for x in OUT_ORDER[i + 1:]],
                                FRONT + turn + 1)
                        for what in WORK[turn]:
                            kind, i = what
                            if kind == "w1":
                                hidden_rows(i)
                            elif kind == "PV":
                                weighted_values(i)
                            else:
                                o = vacant(what)
                                if kind == "pe":
                                    pe.wait_ge(pe_in, 32)
                                    ins = nc.tensor.transpose(o[:, 0:2 * CMP_BLOCK], pe_rows[:, :],
                                                              ident[0:2 * CMP_BLOCK, 0:2 * CMP_BLOCK])
                                elif kind == "pair":
                                    ins = transpose_pair(i, o)
                                elif kind == "logit":
                                    ins = logits(i, o)
                                elif kind == "kv":
                                    ins = compressed_kv(o)
                                elif kind == "csc":
                                    ins = compressed_scores(o)
                                elif kind == "pct":
                                    ins = compressed_weights(o)
                                elif kind == "S":
                                    ins = scores(i, o)
                                elif kind == "T":
                                    ins = transposed_weights(i, o)
                                ins.then_inc(bank_ready[USE[what] % 3], 1)

                    def transpose_hidden(j):
                        pe.wait_ge(h_ready, j)
                        for c in range(4):
                            for t in range(NT):
                                ins = nc.tensor.transpose(
                                    bank[4 + c // 2][:, (2 * (c % 2) + t) * P:(2 * (c % 2) + t + 1) * P],
                                    hrow[:, t, c * P:(c + 1) * P], ident)
                        ins.then_inc(ht_ready, 1)

                    def turn(j, first):
                        for i in range(2 * CPB):
                            if i == 0 and not first:
                                pe.wait_ge(silu_done, j)
                            if i == CPB and not first:
                                transpose_hidden(j)
                            if i < CPB and first:
                                pe.wait_ge(nt_lo, KC // 2 + i + 1)
                            mm3(i, bank[2 * (i // CPB):2 * (i // CPB) + 2], x_lhs, 2 * (i % CPB), N,
                                i % CPB == 0, i % CPB == CPB - 1, 2 * CPB * j + (FF_0 + i + 1))
                            if i + AHEAD < CPB and first:
                                x_T(KC // 2, i + AHEAD)
                        if not first:
                            pe.wait_ge(ht_lo, j)

                    pe.wait_ge(y_ev, 2 * OUT_BLOCKS)
                    pe.wait_ge(ysq_done, 2 * OUT_BLOCKS)
                    for b in range(AHEAD):
                        x_T(KC // 2, b)
                    turn(0, True)
                    with pe.Fori(1, FF_BLOCKS) as j:
                        turn(j, False)

                    for it in range(OUT_BLOCKS // 2):
                        for i in range(2 * DN_CHUNKS):
                            b = i // DN_CHUNKS
                            if it == 0 and i == 0:
                                pe.wait_ge(silu_done, FF_BLOCKS)
                            if it == 0 and i == 5:
                                transpose_hidden(FF_BLOCKS)
                            if it == 0 and i == DN_CHUNKS - 2:
                                pe.wait_ge(ht_lo, FF_BLOCKS)
                            if i % DN_CHUNKS == 0:
                                pe.wait_ge(y_ev, 4 * it + 2 * (OUT_BLOCKS - 1 + b))
                                pe.wait_ge(ysq_done, 4 * it + 2 * (OUT_BLOCKS - 1 + b))
                            mm3(i, bank[2 * b:2 * b + 2], h_lhs, 2 * (i % DN_CHUNKS), N,
                                i % DN_CHUNKS == 0, i % DN_CHUNKS == DN_CHUNKS - 1,
                                2 * DN_CHUNKS * it + (DN_0 + i + 1))

            nc.gpsimd.sem_clear(range(sems[0].num, sems[-1].num + 1))
            nc.all_engine_barrier()

        with nc.Block() as block:
            @block.sync
            def _(sp):
                sp.dma_start(out[0].rearrange("(t p) d -> p t d", p=P), X[:]).then_inc(x_out, 16)
                sp.wait_ge(x_out, 16)
                for i in range(RING):
                    sp.wait_ge(first_in[i], 16 * (DEPTH + 1))


_INS = ["x", "w_in", "w_out", "cmp_pe_k", "cmp_w1_k", "cmp_w2_k", "cmp_pe_v", "cmp_w1_v", "cmp_w2_v",
        "w_gate", "w_up", "w_down", "g_pre_mix", "g_post_mix", "g_pre_ffn", "g_post_ffn"]


def kernel(**inputs):
    import numpy as np
    import concourse.bacc as bacc
    from concourse.bass_utils import run_bass_kernel_spmd

    nc = bacc.Bacc("TRN2", target_bir_lowering=False, num_devices=1)
    arrays, args = {}, []
    for name in _INS:
        arrays[f"in_{name}"] = np.ascontiguousarray(inputs[name])
        args.append(nc.dram_tensor(f"in_{name}", arrays[f"in_{name}"].shape, F32, kind="ExternalInput").ap())
    arrays["consts"] = constants()
    args.append(nc.dram_tensor("consts", arrays["consts"].shape, F32, kind="ExternalInput").ap())
    args.append(nc.dram_tensor("out", (1, SEQ, D), F32, kind="ExternalOutput").ap())
    hybrid_trunk(nc, *args)
    r = run_bass_kernel_spmd(nc, [arrays], core_ids=[0])
    return r.results[0]["out"]
```
